# Optimizing a Trainium2 kernel written in Bass

```python
import functools
import jax
import jax.numpy as jnp
from jax import lax
import numpy as np

D_MODEL = 1024
BATCH = 1
SEQ = 512
DEPTH = 2
DEC_BATCH = 8
DEC_SEQ = 1
PAST_LEN = 4096
PAGE_SIZE = 128

A_HEADS = 8
A_NOPE = 64
A_ROPE = 32
A_V = 64
A_Q_LORA = 384
A_KV_LORA = 256
ROPE_BASE = 10000.0
ATT_BLOCK = 128
SM_SCALE = (A_NOPE + A_ROPE) ** -0.5
B_HEADS = 4
B_DK = 128
B_DV = 128
B_CHUNK = 16
C_WIDTH = D_MODEL
C_KERNEL = 3
D_FF = ((8 * D_MODEL // 3 + 127) // 128) * 128
RMS_EPS = 1e-6

N_AB_LAYERS = (DEPTH + 1) // 2
N_C_LAYERS = DEPTH // 2
AB_SPLITS = (A_Q_LORA, A_KV_LORA, A_ROPE, B_HEADS * B_DK, B_HEADS * B_DK, B_HEADS * B_DV, B_HEADS * B_DV)
AB_IN = A_Q_LORA + A_KV_LORA + A_ROPE + 2 * B_HEADS * B_DK + 2 * B_HEADS * B_DV
AB_MIX = A_HEADS * A_V + B_HEADS * B_DV

kernel_name = 'hybrid_mla_hgrn2_shortconv_macaron_step'

def rms_norm(x, g):
    xf = x.astype(jnp.float32)
    y = xf * lax.rsqrt(jnp.mean(xf * xf, axis=-1, keepdims=True) + RMS_EPS)
    return (y * g.astype(jnp.float32)).astype(x.dtype)

def half_ffn(x, g, w_gate, w_up, w_down):
    h = rms_norm(x, g)
    return x + 0.5 * ((jax.nn.silu(h @ w_gate) * (h @ w_up)) @ w_down)

def rope_tables(pos):
    inv = ROPE_BASE ** (-jnp.arange(0, A_ROPE, 2, dtype=jnp.float32) / A_ROPE)
    ang = pos.astype(jnp.float32)[:, None] * inv[None, :]
    return jnp.cos(ang), jnp.sin(ang)

def apply_rope(x, cos, sin):
    cos = cos.astype(x.dtype)
    sin = sin.astype(x.dtype)
    half = A_ROPE // 2
    x1, x2 = x[..., :half], x[..., half:]
    return jnp.concatenate([x1 * cos - x2 * sin, x1 * sin + x2 * cos], axis=-1)

def mla_prompt(q_nope, q_pe, ckv, kpe, w_ukv):
    b, s = ckv.shape[:2]
    kv = (ckv @ w_ukv).reshape(b, s, A_HEADS, A_NOPE + A_V)
    k_nope, v = kv[..., :A_NOPE], kv[..., A_NOPE:]
    nb = s // ATT_BLOCK
    qn = q_nope.reshape(b, nb, ATT_BLOCK, A_HEADS, A_NOPE).swapaxes(0, 1)
    qp = q_pe.reshape(b, nb, ATT_BLOCK, A_HEADS, A_ROPE).swapaxes(0, 1)
    key_pos = jnp.arange(s)

    def block(args):
        qn_b, qp_b, i = args
        sc = (jnp.einsum('bqhn,bkhn->bhqk', qn_b, k_nope)
              + jnp.einsum('bqhr,bkr->bhqk', qp_b, kpe)).astype(jnp.float32) * SM_SCALE
        q_pos = i * ATT_BLOCK + jnp.arange(ATT_BLOCK)
        sc = jnp.where(key_pos[None, :] <= q_pos[:, None], sc, -jnp.inf)
        p = jax.nn.softmax(sc, axis=-1).astype(v.dtype)
        return jnp.einsum('bhqk,bkhv->bqhv', p, v)

    o = lax.map(block, (qn, qp, jnp.arange(nb)))
    return o.swapaxes(0, 1).reshape(b, s, A_HEADS * A_V)

def mla_sample(q_nope, q_pe, ckv, kpe, pool_ckv, pool_kpe, layer_idx, page_table, w_ukv):
    db, ds = ckv.shape[:2]
    w = w_ukv.reshape(A_KV_LORA, A_HEADS, A_NOPE + A_V)
    w_uk, w_uv = w[..., :A_NOPE], w[..., A_NOPE:]
    q_lat = jnp.einsum('bshn,chn->bshc', q_nope, w_uk)
    ckv_past = pool_ckv[layer_idx, page_table].reshape(db, -1, A_KV_LORA)
    kpe_past = pool_kpe[layer_idx, page_table].reshape(db, -1, A_ROPE)
    n_past = ckv_past.shape[1]
    sc_past = (jnp.einsum('bshc,btc->bhst', q_lat, ckv_past)
               + jnp.einsum('bshr,btr->bhst', q_pe, kpe_past)).astype(jnp.float32) * SM_SCALE
    sc_self = (jnp.einsum('bshc,btc->bhst', q_lat, ckv)
               + jnp.einsum('bshr,btr->bhst', q_pe, kpe)).astype(jnp.float32) * SM_SCALE
    causal = jnp.tril(jnp.ones((ds, ds), dtype=bool))
    sc_self = jnp.where(causal, sc_self, -jnp.inf)
    p = jax.nn.softmax(jnp.concatenate([sc_past, sc_self], axis=-1), axis=-1).astype(ckv.dtype)
    o_lat = (jnp.einsum('bhst,btc->bshc', p[..., :n_past], ckv_past)
             + jnp.einsum('bhst,btc->bshc', p[..., n_past:], ckv))
    o = jnp.einsum('bshc,chv->bshv', o_lat, w_uv)
    return o.reshape(db, ds, A_HEADS * A_V)

def hgrn2(q_raw, f_raw, i_raw, g_raw, lb, g_out, s0):
    b, L = q_raw.shape[:2]
    f32 = jnp.float32
    q = jax.nn.silu(q_raw.astype(f32)) * B_DK ** -0.5
    f = lb + (1.0 - lb) * jax.nn.sigmoid(f_raw.astype(f32))
    k = 1.0 - f
    logf = jnp.log(f)
    v = i_raw.astype(f32)
    pad = (-L) % B_CHUNK
    n = (L + pad) // B_CHUNK

    def blocks(t, d):
        t = jnp.pad(t, ((0, 0), (0, pad), (0, 0)))
        return t.reshape(b, n, B_CHUNK, B_HEADS, d)

    q, k, logf, v = blocks(q, B_DK), blocks(k, B_DK), blocks(logf, B_DK), blocks(v, B_DV)
    bcum = jnp.cumsum(logf, axis=2)
    qe = q * jnp.exp(bcum)
    ke = k * jnp.exp(-bcum)
    kd = k * jnp.exp(bcum[:, :, -1:] - bcum)
    decay = jnp.exp(bcum[:, :, -1])
    causal = jnp.tril(jnp.ones((B_CHUNK, B_CHUNK), dtype=bool))
    att = jnp.where(causal, jnp.einsum('bntha,bnsha->bnhts', qe, ke), 0.0)
    o_intra = jnp.einsum('bnhts,bnshv->bnthv', att, v)

    def step(S, xs):
        qe_c, kd_c, v_c, dec_c = xs
        o_c = jnp.einsum('btha,bhav->bthv', qe_c, S)
        S = dec_c[..., None] * S + jnp.einsum('btha,bthv->bhav', kd_c, v_c)
        return S, o_c

    s_fin, o_inter = lax.scan(step, s0, (qe.swapaxes(0, 1), kd.swapaxes(0, 1), v.swapaxes(0, 1), decay.swapaxes(0, 1)))
    o = (o_intra + o_inter.swapaxes(0, 1)).reshape(b, n * B_CHUNK, B_HEADS, B_DV)[:, :L]
    o = o * lax.rsqrt(jnp.mean(o * o, axis=-1, keepdims=True) + RMS_EPS) * g_out.astype(f32)
    gate = jax.nn.silu(g_raw.astype(f32)).reshape(b, L, B_HEADS, B_DV)
    return (o * gate).reshape(b, L, B_HEADS * B_DV).astype(q_raw.dtype), s_fin

def ab_mixer(h, cos, sin, s0, attend, w_in, g_q, g_kv, w_uq, lb, g_out, w_out):
    b, L = h.shape[:2]
    cuts = [int(c) for c in np.cumsum(AB_SPLITS)[:-1]]
    c_q, c_kv, k_pe, q_b, f_b, i_b, g_b = jnp.split(h @ w_in, cuts, axis=-1)
    cq = rms_norm(c_q, g_q)
    q = (cq @ w_uq).reshape(b, L, A_HEADS, A_NOPE + A_ROPE)
    q_nope = q[..., :A_NOPE]
    q_pe = apply_rope(q[..., A_NOPE:], cos[:, None], sin[:, None])
    ckv = rms_norm(c_kv, g_kv)
    kpe = apply_rope(k_pe, cos, sin)
    o_a = attend(q_nope, q_pe, ckv, kpe)
    o_b, s_new = hgrn2(q_b, f_b, i_b, g_b, lb, g_out, s0)
    y = jnp.concatenate([o_a, o_b], axis=-1) @ w_out
    return y, ckv, kpe, s_new

def c_mixer(h, buf, w_in, w_conv, w_out):
    bg, cg, u = jnp.split(h @ w_in, 3, axis=-1)
    v = cg * u
    L = v.shape[1]
    ext = jnp.concatenate([buf.astype(v.dtype), v], axis=1)
    y = w_conv[0] * ext[:, 0:L]
    for tap in range(1, C_KERNEL):
        y = y + w_conv[tap] * ext[:, tap:tap + L]
    return (bg * y) @ w_out, ext[:, L:]

def setup_inputs(seed: int = 0) -> dict:
    key = jax.random.key(seed)
    ks = jax.random.split(key, 24)
    f32 = jnp.float32
    n_pages = PAST_LEN // PAGE_SIZE
    n_pool = (DEC_BATCH * n_pages * 5) // 4

    def w(k, shape, fan_in):
        return jax.random.normal(k, shape, f32) * (fan_in ** -0.5)

    def gain(k, shape):
        return 1.0 + 0.05 * jax.random.normal(k, shape, f32)

    page_table = jax.random.permutation(ks[6], n_pool)[:DEC_BATCH * n_pages].reshape(DEC_BATCH, n_pages).astype(jnp.int32)
    return {
        'x_prompt': jax.random.normal(ks[0], (BATCH, SEQ, D_MODEL), f32),
        'x_sample': jax.random.normal(ks[1], (DEC_BATCH, DEC_SEQ, D_MODEL), f32),
        'cache_ckv': jax.random.normal(ks[2], (N_AB_LAYERS, n_pool, PAGE_SIZE, A_KV_LORA), f32),
        'cache_kpe': jax.random.normal(ks[3], (N_AB_LAYERS, n_pool, PAGE_SIZE, A_ROPE), f32),
        'state_hgrn': 0.5 * jax.random.normal(ks[4], (N_AB_LAYERS, DEC_BATCH, B_HEADS, B_DK, B_DV), f32),
        'state_conv': jax.random.normal(ks[5], (N_C_LAYERS, DEC_BATCH, C_KERNEL - 1, C_WIDTH), f32),
        'page_table': page_table,
        'norm_g': gain(ks[7], (DEPTH, 3, D_MODEL)),
        'final_norm_g': gain(ks[8], (D_MODEL,)),
        'w_ffn_gate': w(ks[9], (DEPTH, 2, D_MODEL, D_FF), D_MODEL),
        'w_ffn_up': w(ks[10], (DEPTH, 2, D_MODEL, D_FF), D_MODEL),
        'w_ffn_down': w(ks[11], (DEPTH, 2, D_FF, D_MODEL), D_FF),
        'w_in_ab': w(ks[12], (N_AB_LAYERS, D_MODEL, AB_IN), D_MODEL),
        'g_q_lora': gain(ks[13], (N_AB_LAYERS, A_Q_LORA)),
        'g_kv_lora': gain(ks[14], (N_AB_LAYERS, A_KV_LORA)),
        'w_uq': w(ks[15], (N_AB_LAYERS, A_Q_LORA, A_HEADS * (A_NOPE + A_ROPE)), A_Q_LORA),
        'w_ukv': w(ks[16], (N_AB_LAYERS, A_KV_LORA, A_HEADS * (A_NOPE + A_V)), A_KV_LORA),
        'hgrn_lower_bound': 0.1 * jax.random.normal(ks[17], (DEPTH + 1, B_HEADS * B_DK), f32),
        'g_hgrn_out': gain(ks[18], (N_AB_LAYERS, B_DV)),
        'w_out_ab': w(ks[19], (N_AB_LAYERS, AB_MIX, D_MODEL), AB_MIX),
        'w_in_c': w(ks[20], (N_C_LAYERS, D_MODEL, 3 * C_WIDTH), D_MODEL),
        'w_conv_c': w(ks[21], (N_C_LAYERS, C_KERNEL, C_WIDTH), C_KERNEL),
        'w_out_c': w(ks[22], (N_C_LAYERS, C_WIDTH, D_MODEL), C_WIDTH),
    }

def reference(x_prompt, x_sample, cache_ckv, cache_kpe, state_hgrn, state_conv, page_table,
              norm_g, final_norm_g, w_ffn_gate, w_ffn_up, w_ffn_down,
              w_in_ab, g_q_lora, g_kv_lora, w_uq, w_ukv, hgrn_lower_bound, g_hgrn_out, w_out_ab,
              w_in_c, w_conv_c, w_out_c):
    b_p, s_p = x_prompt.shape[:2]
    s_d = x_sample.shape[1]
    past_len = page_table.shape[1] * cache_ckv.shape[2]
    cos_p, sin_p = rope_tables(jnp.arange(s_p))
    cos_d, sin_d = rope_tables(past_len + jnp.arange(s_d))
    lb_all = jnp.cumsum(jax.nn.softmax(hgrn_lower_bound.astype(jnp.float32), axis=0), axis=0)

    xp, xd = x_prompt, x_sample
    ckv_p_l, kpe_p_l, ckv_d_l, kpe_d_l = [], [], [], []
    hg_p_l, hg_d_l, cv_p_l, cv_d_l = [], [], [], []
    for layer in range(DEPTH):
        ffn_a = (w_ffn_gate[layer, 0], w_ffn_up[layer, 0], w_ffn_down[layer, 0])
        ffn_b = (w_ffn_gate[layer, 1], w_ffn_up[layer, 1], w_ffn_down[layer, 1])
        xp = half_ffn(xp, norm_g[layer, 0], *ffn_a)
        xd = half_ffn(xd, norm_g[layer, 0], *ffn_a)
        hp = rms_norm(xp, norm_g[layer, 1])
        hd = rms_norm(xd, norm_g[layer, 1])
        if layer % 2 == 0:
            j = layer // 2
            shared = (w_in_ab[j], g_q_lora[j], g_kv_lora[j], w_uq[j], lb_all[layer], g_hgrn_out[j], w_out_ab[j])
            s0_p = jnp.zeros((b_p, B_HEADS, B_DK, B_DV), jnp.float32)
            attend_p = functools.partial(mla_prompt, w_ukv=w_ukv[j])
            attend_d = functools.partial(mla_sample, pool_ckv=cache_ckv, pool_kpe=cache_kpe,
                                         layer_idx=j, page_table=page_table, w_ukv=w_ukv[j])
            yp, ckv_p, kpe_p, sp = ab_mixer(hp, cos_p, sin_p, s0_p, attend_p, *shared)
            yd, ckv_d, kpe_d, sd = ab_mixer(hd, cos_d, sin_d, state_hgrn[j].astype(jnp.float32), attend_d, *shared)
            ckv_p_l.append(ckv_p)
            kpe_p_l.append(kpe_p)
            ckv_d_l.append(ckv_d)
            kpe_d_l.append(kpe_d)
            hg_p_l.append(sp.astype(x_prompt.dtype))
            hg_d_l.append(sd.astype(x_sample.dtype))
        else:
            j = layer // 2
            buf_p = jnp.zeros((b_p, C_KERNEL - 1, C_WIDTH), xp.dtype)
            yp, bp = c_mixer(hp, buf_p, w_in_c[j], w_conv_c[j], w_out_c[j])
            yd, bd = c_mixer(hd, state_conv[j], w_in_c[j], w_conv_c[j], w_out_c[j])
            cv_p_l.append(bp)
            cv_d_l.append(bd)
        xp = xp + yp
        xd = xd + yd
        xp = half_ffn(xp, norm_g[layer, 2], *ffn_b)
        xd = half_ffn(xd, norm_g[layer, 2], *ffn_b)

    y_prompt = rms_norm(xp, final_norm_g)
    y_sample = rms_norm(xd, final_norm_g)
    return (y_prompt, y_sample,
            jnp.stack(ckv_p_l), jnp.stack(kpe_p_l), jnp.stack(ckv_d_l), jnp.stack(kpe_d_l),
            jnp.stack(hg_p_l), jnp.stack(hg_d_l), jnp.stack(cv_p_l), jnp.stack(cv_d_l))


_drawn_inputs = setup_inputs


def setup_inputs(seed=0):
    import zlib

    import numpy as np

    out = dict(_drawn_inputs(seed))
    spreads = {}
    factors = {'cache_ckv': 2.826, 'cache_kpe': 5.191, 'g_q_lora': 8.0}
    for name, (base, spread) in spreads.items():
        noise = np.random.default_rng([zlib.crc32(name.encode()), seed]).standard_normal(out[name].shape)
        drawn = base * np.exp(spread * noise) if base else spread * noise
        out[name] = jnp.asarray(drawn.astype(out[name].dtype))
    for name, factor in factors.items():
        out[name] = (out[name] * factor).astype(out[name].dtype)
    return out
```

```python
from contextlib import ExitStack

import numpy as np

import concourse.bass as bass
from concourse import mybir
from concourse.alu_op_type import AluOpType as ALU

F32 = mybir.dt.float32
F32R = mybir.dt.float32r
I32 = mybir.dt.int32
ACT = mybir.ActivationFunctionType
AX = mybir.AxisListType

P = 128
D_MODEL, SEQ, BATCH_D, D_FF = 1024, 512, 8, 2816
NP_TOK = SEQ
NT = SEQ + BATCH_D
HALF = NT // 2
KC = D_MODEL // P
FC = D_FF // P
HEADS, NOPE, ROPE, VDIM, Q_LORA, KV_LORA = 8, 64, 32, 64, 384, 256
QC, CC = Q_LORA // P, KV_LORA // P
BH, DK = 4, 128
CHUNK = 16
PAGE, PAGES, POOL = 128, 32, 320
SM_SCALE = (NOPE + ROPE) ** -0.5
EPS = 1e-6
NEG = -1e30

UNIT = 8 * P
DOWN_U = 3
GATE_UNITS = 2 * FC
FFN_UNITS = GATE_UNITS + KC * DOWN_U
FFN_GROUPS = GATE_UNITS + KC
AB_UNITS = 22
Z_Q, Z_G, Z_F, Z_I, Z_CQ, Z_CKV, Z_KPE = 0, 4, 8, 12, 16, 19, 21
UQ_UNITS, UKV_UNITS = 3, 2
C_UNITS = 3 * KC

PHASES = [("ffn0", FFN_UNITS, FFN_GROUPS), ("ab", AB_UNITS, AB_UNITS), ("uq", UQ_UNITS, HEADS),
          ("ukv", UKV_UNITS, 0), ("ab_out", KC, KC), ("ffn1", FFN_UNITS, FFN_GROUPS),
          ("ffn2", FFN_UNITS, FFN_GROUPS), ("c", C_UNITS, C_UNITS), ("c_out", KC, KC),
          ("ffn3", FFN_UNITS, FFN_GROUPS)]
U0, G0 = {}, {}
_u = _g = 0
for _name, _units, _groups in PHASES:
    U0[_name], G0[_name] = _u, _g
    _u, _g = _u + _units, _g + _groups
N_UNITS = _u
BLOCKS = SEQ // P
CH_BLK = P // CHUNK
GRP = 4
T_W = 2 * P + ROPE
T_SLOTS, N_SLOTS = 3, 3
assert N_UNITS % 3 == 0
READS = {"ffn0": 0, "ab": 1, "ffn1": 2, "ffn2": 3, "c": 4, "ffn3": 5}
FFN_NO = {"ffn0": 0, "ffn1": 1, "ffn2": 2, "ffn3": 3}

C_IDENT, C_ONES, C_ROPE, C_CAUSAL, C_INTRA, C_CHUNK, C_EPS, C_W = 0, 128, 256, 776, 904, 1032, 1040, 1041
G_NORM, G_FINAL, G_Q, G_KV, G_LB, G_OUT, G_CONV, G_W = 0, 48, 56, 59, 61, 73, 74, 98


def build(nc, dram):
    ctx = ExitStack()
    with ctx:
        sems = {}

        def S(name):
            if name not in sems:
                sems[name] = ctx.enter_context(nc.semaphore(name))
            return sems[name]

        top = [(nc.sbuf_base + 31) // 32 * 32]

        def tile(name, shape, dt=F32, offset=None):
            size = int(np.prod(shape[1:])) * 4
            if offset is None:
                offset = top[0]
                top[0] += (size + 31) // 32 * 32
            return nc.alloc_sbuf_tensor_at(f"sb_{name}", shape, dt, offset=offset)

        TOK = NT * 4
        x = tile("x", [P, KC, NT])
        raw = [tile(f"raw{i}", [P, 8, P]) for i in range(3)]
        w_hi = [tile(f"w_hi{i}", [P, 8, P], F32R) for i in range(3)]
        w_lo = [tile(f"w_lo{i}", [P, 8, P], F32R) for i in range(3)]
        at_t = top[0]
        t1, t2, t3, acc = [tile(n, [P, NT]) for n in ("t1", "t2", "t3", "acc")]
        r = tile("r", [P, NT])
        cst = tile("cst", [P, C_W])
        gain = tile("gain", [P, G_W])
        pages = tile("pages", [1, BATCH_D * PAGES], I32)
        conv_st = tile("conv_st", [P, KC, 2, BATCH_D])
        k_pe = tile("k_pe", [P, NT])
        rope_r = tile("rope_r", [P, NT])
        lb = tile("lb", [P, 4, BH])
        at_h = top[0]
        h_hi = tile("h_hi", [P, KC, NT], F32R)
        h_lo = tile("h_lo", [P, KC, NT], F32R)
        at_a = top[0]
        a_hi = tile("a_hi", [P, FC, NT], F32R)
        a_lo = tile("a_lo", [P, FC, NT], F32R)
        at_e = top[0]

        def tiles_at(start, *specs):
            out = []
            for name, shape, *dt in specs:
                out.append(tile(name, shape, dt[0] if dt else F32, offset=start))
                start += (int(np.prod(shape[1:])) * 4 + 31) // 32 * 32
            assert start <= nc.sbuf_usable_end, (name, start, nc.sbuf_usable_end)
            return out

        m_hi, m_lo = tiles_at(at_a + 28 * TOK, ("m_hi", [P, KC, NT], F32R), ("m_lo", [P, KC, NT], F32R))
        z, = tiles_at(at_a, ("z", [P, AB_UNITS, NT]))
        k_all, bcum, qe, ke, kd = tiles_at(at_a + 22 * TOK, ("k_all", [P, BH, NT]), ("bcum", [P, BH, SEQ]),
                                           ("qe", [P, BH, SEQ]), ("ke", [P, BH, SEQ]), ("kd", [P, BH, SEQ]))
        v_blk = tiles_at(at_a + 26 * TOK, ("v_blk0", [P, CH_BLK, P]), ("v_blk1", [P, CH_BLK, P]))
        o_fac, = tiles_at(at_a + 26 * TOK, ("o_fac", [P, BH, NT]))
        q_t, k_t, v_t, prob, prob_t = tiles_at(at_a, ("q_t", [P, HEADS, NT]), ("k_t", [P, HEADS, SEQ]),
                                               ("v_t", [P, BLOCKS, HEADS * VDIM]), ("prob", [P, 10, P]), ("prob_t", [P, 10, P]))
        cq_hi, cq_lo, ckv_hi, ckv_lo, squares = tiles_at(
            at_h, ("cq_hi", [P, QC, NT], F32R), ("cq_lo", [P, QC, NT], F32R), ("ckv_hi", [P, CC, NT], F32R),
            ("ckv_lo", [P, CC, NT], F32R), ("squares", [P, 4, NT]))
        st0, st1, v_diag, s_tmp = tiles_at(at_h + 10 * TOK, ("st0", [P, BH, P]), ("st1", [P, BH, P]),
                                           ("v_diag", [P, BH, P]), ("s_tmp", [P, BH, P]))
        st = [st0, st1]
        ckv, = tiles_at(at_h + 14 * TOK, ("ckv", [P, CC, NT]))
        c_slots = tiles_at(at_h, *[(f"lat_t{i}", [P, GRP, T_W]) for i in range(T_SLOTS)],
                           *[(f"lat{i}", [P, GRP, KV_LORA]) for i in range(N_SLOTS)])
        lat_t, lat = c_slots[:T_SLOTS], c_slots[T_SLOTS:]
        s_ring, kdv0, kdv1, att0, att1, decay = tiles_at(
            at_e, ("s_ring", [P, 2 * CH_BLK, P]), ("kdv0", [P, 2, P]), ("kdv1", [P, 2, P]), ("att0", [P, P]),
            ("att1", [P, P]), ("decay", [P, BH, SEQ // CHUNK]))
        kdv, att = [kdv0, kdv1], [att0, att1]
        (w_uv, kc0, kc1, kp0, kp1, sc, pr, q_lat, q_pe4, o_lat, self_row, small, mx_p, sum_p) = tiles_at(
            at_e, ("w_uv", [P, CC, HEADS, VDIM]), ("kc0", [P, GRP, ROPE]), ("kc1", [P, GRP, ROPE]), ("kp0", [P, P]), ("kp1", [P, P]), ("sc", [P, PAGES + 1, HEADS]),
            ("pr", [P, PAGES + 1, HEADS]), ("q_lat", [P, BATCH_D, CC, HEADS]), ("q_pe4", [P, BATCH_D, GRP * HEADS]),
            ("o_lat", [P, CC, HEADS, BATCH_D]), ("self_row", [P, CC * P]), ("small", [P, 6, HEADS]),
            ("mx_p", [P, 2, BLOCKS]), ("sum_p", [P, 2, BLOCKS]))
        kp, kc = [kp0, kp1], [kc0, kc1]
        s_fin, = tiles_at(at_t, ("s_fin", [P, BH, P]))
        w_uk, = tiles_at(at_t, ("w_uk", [NOPE, HEADS, KV_LORA]))
        v_ext, c_tail, c_last = tiles_at(at_a, ("v_ext", [P, 2 + NT]), ("c_tail", [P, KC, 2]), ("c_last", [P, KC, BATCH_D]))

        bank = [ctx.enter_context(nc.psum_tensor(f"bank{i}", [P, 512], F32)) for i in range(8)]
        ident = cst[:, C_IDENT:C_IDENT + P]
        ones = cst[:, C_ONES:C_ONES + P]

        half = [slice(0, HALF), slice(HALF, NT)]

        def pair(g, hf):
            return bank[2 * (g % 3) + hf][:, 0:HALF]

        def split_hi(n0, step=None):
            n = n0 if step is None else n0 + step
            slot = n0 % 3
            nc.scalar.wait_ge(S(f"w_loaded{slot}"), 16 * (n0 // 3 + 1) if step is None else 16 * (n0 // 3 + 1) + step_loads(step))
            if step is not None or n0 >= 3:
                nc.scalar.wait_ge(S("half_done"), 2 * n - 4)
            nc.scalar.activation(w_hi[slot][:], raw[slot][:], ACT.Copy).then_inc(S("w_hi_done"), 1)

        def split_lo(n0, step=None):
            n = n0 if step is None else n0 + step
            slot = n0 % 3
            nc.vector.wait_ge(S("w_hi_done"), n + 1)
            nc.vector.tensor_tensor(w_lo[slot][:], raw[slot][:], w_hi[slot][:], ALU.subtract).then_inc(S("w_lo_done"), 1)

        def step_loads(step):
            return step.loads

        class Step:

            def __init__(self, i, k):
                assert k % 3 == 0
                self.i, self.k = i, k
                self.loads = i * (16 * k // 3)

            def __radd__(self, n):
                return n + self.i * self.k

        def multiply(slot, g, hi, lo, k0, chunks, first, last, wait_chunk=None):
            for hf in range(2):
                out = pair(g, hf)
                for c in range(chunks):
                    if wait_chunk:
                        wait_chunk(c, hf)
                    xh, xl = hi[:, k0 + c, half[hf]], lo[:, k0 + c, half[hf]]
                    wh, wl = w_hi[slot][:, c, :], w_lo[slot][:, c, :]
                    nc.tensor.matmul(out, wh, xh, start=first and c == 0, stop=False)
                    nc.tensor.matmul(out, wh, xl, start=False, stop=False)
                    mm = nc.tensor.matmul(out, wl, xh, start=False, stop=last and c == chunks - 1)
                mm.then_inc(S("half_done"), 1)

        def unit_ready(n):
            nc.tensor.wait_ge(S("w_lo_done"), n + 1)

        def group_free(g):
            nc.tensor.wait_ge(S("drained"), 2 * g - 4)

        def norm_sum(res):
            for hf in range(2):
                nc.tensor.wait_ge(S("squares_added"), 14 * res + 13 + hf)
                nc.tensor.matmul(bank[6 + hf][:, 0:HALF], ones, acc[:, half[hf]], start=True, stop=True) \
                    .then_inc(S("norm_summed"), 1)

        def inverse_root(out, sums, n, width):
            nc.scalar.activation(out, sums, ACT.Ln, bias=cst[:, C_EPS:C_EPS + 1], scale=1.0 / width) \
                .then_inc(S("log_taken"), 1)
            nc.scalar.wait_ge(S("log_taken"), n + 1)
            nc.scalar.activation(out, out, ACT.Exp, scale=-0.5).then_inc(S("factor"), 1)

        def norm_factor(res):
            for hf in range(2):
                nc.scalar.wait_ge(S("norm_summed"), 2 * res + hf + 1)
                inverse_root(r[:, half[hf]], bank[6 + hf][:, 0:HALF], factors_before(res) + hf, D_MODEL)

        def factors_before(res):
            return 2 * res + (4 if res > 1 else 0)

        def factor_ready(res):
            nc.vector.wait_ge(S("factor"), factors_before(res) + 2)

        def chunk_act(res, d, dd, split=True):
            for hf in range(2):
                n = res * 16 + 2 * dd + hf + 1
                if res:
                    nc.scalar.wait_ge(S("x_added"), n - 16)
                src = x[:, dd, half[hf]]
                if split:
                    nc.scalar.activation(h_hi[:, dd, half[hf]], src, ACT.Copy,
                                         scale=gain[:, bass.ds(G_NORM + 8 * res + dd, 1)]).then_inc(S("h_hi_done"), 1)
                to = acc if isinstance(d, int) and d == 0 else t2
                if not res and d >= 2:
                    nc.scalar.wait_ge(S("squares_added"), 2 * (d - 2) + hf + 1)
                nc.scalar.activation(to[:, half[hf]], src, ACT.Square).then_inc(S("squared"), 1)

        def chunk_dve(res, d, dd, split=True):
            for hf in range(2):
                n = res * 16 + 2 * dd + hf + 1
                if split:
                    nc.vector.wait_ge(S("h_hi_done"), n)
                    nc.vector.scalar_tensor_tensor(h_lo[:, dd, half[hf]], x[:, dd, half[hf]],
                                                   gain[:, bass.ds(G_NORM + 8 * res + dd, 1)],
                                                   h_hi[:, dd, half[hf]], op0=ALU.mult, op1=ALU.subtract) \
                        .then_inc(S("h_lo_done"), 1)
                nc.vector.wait_ge(S("squared"), n)
                if not (isinstance(d, int) and d == 0):
                    nc.vector.tensor_tensor(acc[:, half[hf]], acc[:, half[hf]], t2[:, half[hf]], ALU.add) \
                        .then_inc(S("squares_added"), 1)

        def add_residual(res, dd, g, n_last, scaled):
            for hf in range(2):
                xs = x[:, dd, half[hf]]
                nc.vector.wait_ge(S("half_done"), 2 * n_last + hf + 1)
                if scaled:
                    nc.vector.scalar_tensor_tensor(t1[:, half[hf]], pair_at(g, hf), 0.5, r[:, half[hf]],
                                                   op0=ALU.mult, op1=ALU.mult).then_inc(S("drained"), 1)
                else:
                    nc.vector.tensor_copy(t1[:, half[hf]], pair_at(g, hf)).then_inc(S("drained"), 1)
            for hf in range(2):
                xs = x[:, dd, half[hf]]
                nc.vector.wait_ge(S("drained"), 2 * g[1] + hf + 1)
                nc.vector.tensor_tensor(xs, xs, t1[:, half[hf]], ALU.add).then_inc(S("x_added"), 1)

        def pair_at(g, hf):
            return pair(g[0], hf)

        def at(static, moving=0):
            return (static, static + moving)

        def over(eng, peel, total, per, body, tail=0):
            for d in range(peel):
                body(d, 1, 0)
            assert (total - peel - tail) % per == 0
            with eng.Fori(0, (total - peel - tail) // per) as i:
                body(peel, per, i)
            for d in range(total - tail, total):
                body(d, 1, 0)

        block = ctx.enter_context(nc.Block())
        GATE_PEEL, OUT_PEEL, C_PEEL, Z_PEEL = 1, 2, 1, 1
        LAST = "ffn3"
        IN_PHASES = ("ffn0", "ab", "ab_out", "ffn1", "ffn2", "c", "c_out", "ffn3")

        def tail(name):
            return 3 if name == LAST else 0

        def o_block(h, b):
            return slice(b * P, (b + 1) * P)

        def tri(b):
            return b * (b + 1) // 2

        score_at = [bank[5][:, 0:P], bank[5][:, P:3 * P], bank[6][:, 0:3 * P], bank[7][:, 0:4 * P]]

        @block.sync
        def _(sp):
            def stream(n_first, n_end):
                with sp.Fori(0, (n_end - n_first) // 3) as i:
                    for k in range(3):
                        sp.wait_ge(S("w_lo_done"), 3 * i + (n_first + k - 2))
                        sp.dma_start(raw[k][:].rearrange("p c m -> p (c m)"), dram["w"][3 * i + (n_first + k)]) \
                            .then_inc(S(f"w_loaded{k}"), 16)

            sp.dma_start(x[:], dram["x"]).then_inc(S("x_loaded"), 16)
            sp.dma_start(gain[:], dram["gain"]).then_inc(S("gain_loaded"), 16)
            for n in range(3):
                sp.dma_start(raw[n][:].rearrange("p c m -> p (c m)"), dram["w"][n]).then_inc(S(f"w_loaded{n}"), 16)
            sp.dma_start(cst[:], dram["cst"]).then_inc(S("cst_loaded"), 16)
            sp.dma_start(pages[:], dram["pages"]).then_inc(S("pages_loaded"), 16)

            n_cache = -(-(U0["ab_out"] + 3) // 3) * 3
            stream(3, n_cache)
            sp.wait_ge(S("pages_loaded"), 16)
            sp.wait_ge(S("v_kept"), BLOCKS)
            sp.wait_ge(S("k_done"), HEADS)
            for b in range(BATCH_D):
                for kind, slots, width, lo in (("lat_t", lat_t, T_W, 0), ("lat", lat, KV_LORA, T_W)):
                    for g in range(PAGES // GRP):
                        n = b * (PAGES // GRP) + g
                        slot = n % len(slots)
                        if n >= len(slots):
                            sp.wait_ge(S(f"{kind}_used"), n - len(slots) + 1)
                        for j in range(GRP):
                            at_page = b * PAGES + g * GRP + j
                            page = sp.value_load(pages[0:1, at_page:at_page + 1], min_val=0, max_val=POOL - 1)
                            sp.dma_start(slots[slot][:, j, :],
                                         dram["cache"][bass.ds(page, 1), :, lo:lo + width].rearrange("a p w -> (a p) w")) \
                                .then_inc(S(f"{kind}_loaded{slot}_{j}"), 16)
            stream(n_cache, N_UNITS)
            for n in range(KC):
                sp.wait_ge(S("y_ready"), n + 1)
                sp.dma_start(dram["y"][:, n], x[:, n, :]).then_inc(S("y_stored"), 16)
            sp.wait_ge(S("y_stored"), 16 * KC)

        @block.gpsimd
        def _(pool):
            for i in range(2):
                pool.memset(att[i][:], 0.0).then_inc(S("att_zeroed"), 1)
            pool.dma_start(conv_st[:], dram["conv_st"]).then_inc(S("conv_st_loaded"), 16)
            pool.wait_ge(S("conv_st_loaded"), 16)
            pool.dma_start(dram["conv_s"][:, :, 0, :], conv_st[:, :, 1, :]).then_inc(S("conv_old_stored"), 16)
            pool.wait_ge(S("drained"), 2 * (G0["ab"] + 1))
            pool.dma_start(t3[:, 0:SEQ], dram["scan"]).then_inc(S("scan_loaded"), 16)
            pool.wait_ge(S("ckv_ready"), CC)
            pool.dma_start(dram["ckv"], ckv[:]).then_inc(S("ckv_stored"), 16)
            pool.wait_ge(S("k_pe_step"), 3)
            pool.dma_start(dram["k_pe"], k_pe[NOPE:NOPE + ROPE, :]).then_inc(S("k_pe_stored"), 16)
            for b in range(BATCH_D):
                if b == 0:
                    pool.wait_ge(S("cq_summed"), 4)
                if b >= 2:
                    pool.wait_ge(S("os_mm"), b - 1)
                    pool.wait_ge(S(f"st_stored{b % 2}"), 16 * (b // 2))
                pool.dma_start(st[b % 2][:], dram["state"][b]).then_inc(S(f"st_loaded{b % 2}"), 16)
                if b >= 1:
                    pool.wait_ge(S("s_new"), b)
                    pool.dma_start(dram["state_s"][b - 1], st[(b - 1) % 2][:]).then_inc(S(f"st_stored{(b - 1) % 2}"), 16)
                if b == 0:
                    pool.wait_ge(S("final_kept"), BH)
                    pool.dma_start(dram["state_p"], s_fin[:]).then_inc(S("s_fin_stored"), 16)
            pool.wait_ge(S("s_new"), BATCH_D)
            pool.dma_start(dram["state_s"][BATCH_D - 1], st[1][:]).then_inc(S("st_stored1"), 16)
            pool.wait_ge(S("q_ready"), 2 * HEADS)
            pool.dma_start(w_uk[:], dram["w_uk"]).then_inc(S("w_uk_loaded"), 16)
            pool.dma_start(w_uv[:], dram["w_uv"]).then_inc(S("w_uv_loaded"), 16)
            for t in (q_pe4, sc):
                pool.memset(t[:], 0.0 if t is q_pe4 else NEG).then_inc(S("att_cleared"), 1)
            for n in range(BATCH_D * PAGES // GRP):
                for j in range(GRP):
                    pool.wait_ge(S(f"lat_t_loaded{n % T_SLOTS}_{j}"), 16 * (n // T_SLOTS + 1))
                if n >= 2:
                    pool.wait_ge(S("kp_transposed"), n - 1)
                pool.tensor_copy(kc[n % 2][:], lat_t[n % T_SLOTS][:, :, CC * P:T_W]).then_inc(S("kp_gathered"), 1)
            pool.wait_ge(S("conv_kept"), 2 * KC)
            pool.dma_start(dram["conv_p"], c_tail[:]).then_inc(S("conv_p_stored"), 16)
            pool.dma_start(dram["conv_s"][:, :, 1, :], c_last[:]).then_inc(S("conv_s_stored"), 16)
            for name in ("ckv", "k_pe", "s_fin", "conv_old", "conv_p", "conv_s"):
                pool.wait_ge(S(f"{name}_stored"), 16)
            for i in range(2):
                pool.wait_ge(S(f"st_stored{i}"), 16 * BATCH_D // 2)

        @block.scalar
        def _(act):
            def prefetch(n, step=None):
                if n + 3 < N_UNITS:
                    split_hi(n + 3, step)

            def ffn(name):
                n0, g0, res = U0[name], G0[name], READS[name]

                def gate_up(f0, count, i):
                    st = None if isinstance(i, int) else Step(i, 2 * count)
                    for f in range(f0, f0 + count):
                        ff = f if st is None else f + i * count
                        n, gg = n0 + 2 * f, g0 + 2 * ff
                        if st is None and f == 0:
                            norm_factor(res)
                        prefetch(n, st)
                        for hf in range(2):
                            act.wait_ge(S("drained"), 2 * gg + hf + 1)
                            act.activation(t2[:, half[hf]], t1[:, half[hf]], ACT.Silu).then_inc(S("silu_done"), 1)
                        prefetch(n + 1, st)
                        for hf in range(2):
                            act.wait_ge(S("drained"), 2 * gg + 2 + hf + 1)
                            act.activation(a_hi[:, ff, half[hf]], t3[:, half[hf]], ACT.Copy).then_inc(S("a_hi_done"), 1)

                over(act, GATE_PEEL, FC, 3, gate_up)
                n0 += GATE_UNITS

                def down(d0, count, i):
                    st = None if isinstance(i, int) else Step(i, 3 * count)
                    for d in range(d0, d0 + count):
                        for u in range(DOWN_U):
                            prefetch(n0 + 3 * d + u, st)
                        chunk_act(res + 1, d, d if st is None else d + i * count, split=name != LAST)

                over(act, OUT_PEEL, KC, 3, down, tail(name))

            def out_projection(name, res):
                n0 = U0[name]

                def column(d0, count, i):
                    st = None if isinstance(i, int) else Step(i, count)
                    for d in range(d0, d0 + count):
                        prefetch(n0 + d, st)
                        chunk_act(res, d, d if st is None else d + i * count)

                over(act, OUT_PEEL, KC, 3, column)

            def ab_in():
                n0, g0 = U0["ab"], G0["ab"]

                def column(u0, count, i):
                    st = None if isinstance(i, int) else Step(i, count)
                    for u in range(u0, u0 + count):
                        if st is None:
                            norm_factor(READS["ab"])
                        prefetch(n0 + u, st)

                over(act, Z_PEEL, Z_CQ, 3, column)
                prefetch(n0 + 16)
                for n, z0 in enumerate((Z_Q, Z_G)):
                    act.wait_ge(S("drained"), 2 * (g0 + z0 + BH))
                    act.activation(z[:, z0:z0 + BH, :], z[:, z0:z0 + BH, :], ACT.Silu).then_inc(S("silus"), 1)
                prefetch(n0 + 17)
                act.wait_ge(S("drained"), 2 * (g0 + Z_F + BH))
                act.activation(z[:, Z_F:Z_F + BH, :], z[:, Z_F:Z_F + BH, :], ACT.Sigmoid).then_inc(S("f_sigmoid"), 1)
                prefetch(n0 + 18)
                act.wait_ge(S("f_scaled"), BH)
                act.activation(qe[:], z[:, Z_F:Z_F + BH, 0:SEQ], ACT.Ln).then_inc(S("log_f"), 1)
                prefetch(n0 + 19)
                act.wait_ge(S("cum_done"), BH)
                act.activation(qe[:], bcum[:], ACT.Exp).then_inc(S("exp_cum"), 1)
                act.activation(ke[:], bcum[:], ACT.Exp, scale=-1.0).then_inc(S("exp_cum"), 1)
                prefetch(n0 + 20)
                act.wait_ge(S("to_end"), 1)
                act.activation(kd[:], kd[:], ACT.Exp).then_inc(S("exp_cum"), 1)
                prefetch(n0 + 21)
                for c in range(QC):
                    act.wait_ge(S("drained"), 2 * (g0 + Z_CQ + c + 1))
                    act.activation(cq_hi[:, c, :], z[:, Z_CQ + c, :], ACT.Copy, scale=gain[:, G_Q + c:G_Q + c + 1]) \
                        .then_inc(S("cq_hi_done"), 1)
                    act.activation(squares[:, c, :], z[:, Z_CQ + c, :], ACT.Square).then_inc(S("c_squared"), 1)
                for c in range(CC):
                    act.wait_ge(S("drained"), 2 * (g0 + Z_CKV + c + 1))
                    act.activation(squares[:, 3, :] if c == 0 else acc[:], z[:, Z_CKV + c, :], ACT.Square) \
                        .then_inc(S("c_squared"), 1)
                n = factors_before(1) + 2
                for k, (to, width) in enumerate(((r, Q_LORA), (t3, KV_LORA))):
                    act.wait_ge(S("drained"), 2 * (g0 + AB_UNITS))
                    for hf in range(2):
                        act.wait_ge(S("cq_summed"), 2 * k + hf + 1)
                        inverse_root(to[:, half[hf]], bank[6 + hf][:, 0:HALF], n + 2 * k + hf, width)

            def hgrn():
                def keep(m):
                    act.wait_ge(S("kv_transposed"), m + 1)
                    if m >= 2:
                        act.wait_ge(S("o_mm"), m - 1)
                    act.activation(kdv[m % 2][:].rearrange("p a d -> p (a d)"), bank[m % 2][:, 0:2 * P], ACT.Copy).then_inc(S("kv_kept"), 1)

                keep(0)
                for m in range(BH * BLOCKS):
                    h, b = divmod(m, BLOCKS)
                    if m + 1 < BH * BLOCKS:
                        keep(m + 1)
                    act.wait_ge(S("o_mm"), m + 1)
                    act.activation(z[:, Z_Q + h, o_block(h, b)], bank[6 + m % 2][:, 0:P], ACT.Copy).then_inc(S("o_kept"), 1)
                    if m == 0:
                        act.wait_ge(S("ckv_ready"), CC)
                        act.activation(ckv_hi[:], ckv[:], ACT.Copy).then_inc(S("ckv_hi_done"), 1)
                act.wait_ge(S("os_kept"), 1)
                act.activation(k_all[:], z[:, Z_Q:Z_Q + BH, :], ACT.Square).then_inc(S("o_squared"), 1)
                for h in range(BH):
                    for hf in range(2):
                        act.wait_ge(S("o_summed"), 2 * h + hf + 1)
                        act.activation(o_fac[:, h, half[hf]], bank[2 * h + hf][:, 0:HALF], ACT.Ln,
                                       bias=cst[:, C_EPS:C_EPS + 1], scale=1.0 / DK).then_inc(S("o_log"), 1)
                act.wait_ge(S("o_log"), 2 * BH)
                act.activation(o_fac[:], o_fac[:], ACT.Exp, scale=-0.5).then_inc(S("o_factor"), 1)
                act.wait_ge(S("o_step"), 2)
                act.activation(m_hi[:, BH:, :], z[:, Z_Q:Z_Q + BH, :], ACT.Copy).then_inc(S("mix_hi_done"), 1)

            def qkv():
                n0 = U0["uq"]
                for h in range(HEADS):
                    if h in (2, 5, 7):
                        prefetch(n0 + (2, 5, 7).index(h))
                act.wait_ge(S("k_pe_step"), 3)
                act.wait_ge(S("q_ready"), 1)
                for h in range(HEADS):
                    act.activation(k_t[NOPE:NOPE + ROPE, h, :], k_pe[NOPE:NOPE + ROPE, 0:SEQ], ACT.Copy).then_inc(S("k_kept"), 1)
                for h in range(HEADS):
                    act.wait_ge(S("k_done"), h + 1)
                    act.activation(k_t[0:NOPE, h, :], bank[h % 4][0:NOPE, :], ACT.Copy).then_inc(S("k_kept"), 1)
                for u in range(UKV_UNITS):
                    prefetch(U0["ukv"] + u)

            def attention():
                for i in range(HEADS):
                    def keys(g):
                        n = i * (PAGES // GRP) + g
                        act.wait_ge(S("kp_transposed"), n + 1)
                        if n >= 2:
                            act.wait_ge(S("lat_t_used"), n - 1)
                        act.activation(kp[n % 2][:], bank[1][:, (n % 2) * P:(n % 2 + 1) * P], ACT.Copy).then_inc(S("kp_kept"), 1)

                    def probabilities(b):
                        act.wait_ge(S("max_scaled"), i + 1)
                        if b == 0 and i:
                            act.wait_ge(S("p_transposed"), 3 * i)
                        act.activation(prob[:, tri(b):tri(b + 1), :].rearrange("p a k -> p (a k)"), score_at[b], ACT.Exp,
                                       bias=mx_p[:, 1, b:b + 1], scale=SM_SCALE, accum_out=sum_p[:, 0, b:b + 1]) \
                            .then_inc(S("p_exp"), 1)

                    for g in range(PAGES // GRP):
                        keys(g)
                        if g % 2 == 1:
                            probabilities(g // 2)
                    act.wait_ge(S("self_transposed"), i + 1)
                    act.activation(self_row[0:1, :], bank[1][0:1, 2 * P:4 * P], ACT.Copy).then_inc(S("self_kept"), 1)
                    for e in range(3):
                        act.wait_ge(S("p_transposed"), 3 * i + e + 1)
                        if e == 0 and i:
                            act.wait_ge(S("o_a_mm"), i)
                        size = (4, 4, 2)[e]
                        act.activation(prob_t[:, 4 * e:4 * e + size, :].rearrange("p a k -> p (a k)"),
                                       bank[5 + e][:, 0:size * P], ACT.Copy).then_inc(S("pt_kept"), 1)
                    act.wait_ge(S("sc_shifted"), i + 1)
                    act.activation(pr[:], sc[:], ACT.Exp, scale=SM_SCALE).then_inc(S("pr_exp"), 1)
                    rows = slice(i % 2 * VDIM, (i % 2 + 1) * VDIM)
                    act.wait_ge(S("o_a_mm"), i + 1)
                    act.activation(m_hi[rows, i // 2, 0:SEQ], bank[4][rows, :], ACT.Copy).then_inc(S("oa_hi_done"), 1)
                for i in range(HEADS):
                    rows = slice(i % 2 * VDIM, (i % 2 + 1) * VDIM)
                    act.wait_ge(S("os_a_mm"), 1)
                    act.activation(m_hi[rows, i // 2, SEQ:NT], bank[0][rows, i * BATCH_D:(i + 1) * BATCH_D], ACT.Copy) \
                        .then_inc(S("oa_hi_done"), 1)

            def conv():
                n0, g0 = U0["c"], G0["c"]

                def chunk(j0, count, i):
                    st = None if isinstance(i, int) else Step(i, 3)
                    j = j0
                    jj = j if st is None else j + i
                    if st is None:
                        norm_factor(READS["c"])
                    for u in range(3):
                        prefetch(n0 + 3 * j + u, st)
                        if u == 1:
                            act.wait_ge(S("v_ready"), 2 * jj + 2)
                            act.activation(c_tail[:, jj, :], v_ext[:, SEQ:SEQ + 2], ACT.Copy).then_inc(S("conv_kept"), 1)
                            act.activation(c_last[:, jj, :], v_ext[:, 2 + SEQ:2 + NT], ACT.Copy).then_inc(S("conv_kept"), 1)
                    act.wait_ge(S("c_gated"), jj + 1)
                    act.activation(m_hi[:, jj, :], t1[:], ACT.Copy).then_inc(S("mix_hi_done"), 1)

                over(act, C_PEEL, KC, 1, chunk)

            act.wait_ge(S("x_loaded"), 16)
            act.wait_ge(S("gain_loaded"), 16)
            for d in range(KC):
                chunk_act(0, d, d)
            for n in range(3):
                split_hi(n)
            act.wait_ge(S("lb_step"), 3)
            act.activation(lb[:, 0:3, :], lb[:, 0:3, :], ACT.Exp).then_inc(S("lb_exp"), 1)
            act.wait_ge(S("cst_loaded"), 16)
            ffn("ffn0")
            ab_in()
            hgrn()
            qkv()
            attention()
            out_projection("ab_out", 2)
            ffn("ffn1")
            ffn("ffn2")
            conv()
            out_projection("c_out", 5)
            act.wait_ge(S("conv_p_stored"), 16)
            act.wait_ge(S("conv_s_stored"), 16)
            ffn("ffn3")
            norm_factor(6)

        @block.vector
        def _(dve):
            def prefetch(n, step=None):
                if n + 3 < N_UNITS:
                    split_lo(n + 3, step)

            def ffn(name):
                n0, g0, res, no = U0[name], G0[name], READS[name], FFN_NO[name]

                def gate_up(f0, count, i):
                    st = None if isinstance(i, int) else Step(i, 2 * count)
                    for f in range(f0, f0 + count):
                        ff = f if st is None else f + i * count
                        n, g = n0 + 2 * f, g0 + 2 * f
                        nn = n0 + 2 * ff
                        if st is None and f == 0:
                            factor_ready(res)
                        for hf in range(2):
                            dve.wait_ge(S("half_done"), 2 * nn + hf + 1)
                            dve.tensor_tensor(t1[:, half[hf]], pair(g, hf), r[:, half[hf]], ALU.mult) \
                                .then_inc(S("drained"), 1)
                        prefetch(n, st)
                        for hf in range(2):
                            dve.wait_ge(S("half_done"), 2 * nn + 2 + hf + 1)
                            dve.wait_ge(S("silu_done"), (no * FC + ff) * 2 + hf + 1)
                            dve.tensor_tensor(t3[:, half[hf]], pair(g + 1, hf), t2[:, half[hf]], ALU.mult) \
                                .then_inc(S("drained"), 1)
                        prefetch(n + 1, st)
                        for hf in range(2):
                            dve.wait_ge(S("a_hi_done"), (no * FC + ff) * 2 + hf + 1)
                            dve.tensor_tensor(a_lo[:, ff, half[hf]], t3[:, half[hf]], a_hi[:, ff, half[hf]], ALU.subtract) \
                                .then_inc(S("a_lo_done"), 1)

                over(dve, GATE_PEEL, FC, 3, gate_up)
                n0 += GATE_UNITS
                g0 += GATE_UNITS

                def down(d0, count, i):
                    st = None if isinstance(i, int) else Step(i, 3 * count)
                    for d in range(d0, d0 + count):
                        dd = d if st is None else d + i * count
                        for u in range(DOWN_U - 1):
                            prefetch(n0 + 3 * d + u, st)
                        add_residual(res + 1, dd, (g0 + d, g0 + dd), n0 + 3 * dd + 2, scaled=True)
                        prefetch(n0 + 3 * d + 2, st)
                        chunk_dve(res + 1, d, dd, split=name != LAST)

                over(dve, OUT_PEEL, KC, 3, down, tail(name))

            def out_projection(name, res):
                n0, g0 = U0[name], G0[name]

                def column(d0, count, i):
                    st = None if isinstance(i, int) else Step(i, count)
                    for d in range(d0, d0 + count):
                        dd = d if st is None else d + i * count
                        add_residual(res, dd, (g0 + d, g0 + dd), n0 + dd, scaled=False)
                        prefetch(n0 + d, st)
                        chunk_dve(res, d, dd)

                over(dve, OUT_PEEL, KC, 3, column)

            def ab_in():
                n0, g0 = U0["ab"], G0["ab"]

                def drain(u, uu):
                    for hf in range(2):
                        dve.wait_ge(S("half_done"), 2 * (n0 + uu) + hf + 1)
                        dve.tensor_tensor(z[:, uu, half[hf]], pair(g0 + u, hf), r[:, half[hf]], ALU.mult) \
                            .then_inc(S("drained"), 1)

                def column(u0, count, i):
                    st = None if isinstance(i, int) else Step(i, count)
                    for u in range(u0, u0 + count):
                        if st is None:
                            factor_ready(READS["ab"])
                        drain(u, u if st is None else u + i * count)
                        prefetch(n0 + u, st)

                over(dve, Z_PEEL, Z_CQ, 3, column)
                drain(16, 16)
                prefetch(n0 + 16)
                drain(17, 17)
                prefetch(n0 + 17)
                f_all = z[:, Z_F:Z_F + BH, :]
                dve.wait_ge(S("f_sigmoid"), 1)
                for h in range(BH):
                    dve.tensor_scalar(z[:, Z_F + h, :], z[:, Z_F + h, :], lb[:, 3, h:h + 1], lb[:, 2, h:h + 1], ALU.mult, ALU.add) \
                        .then_inc(S("f_scaled"), 1)
                dve.wait_ge(S("f_scaled"), BH)
                dve.tensor_scalar(k_all[:], f_all, -1.0, 1.0, ALU.mult, ALU.add).then_inc(S("k_all_ready"), 1)
                drain(18, 18)
                prefetch(n0 + 18)
                dve.wait_ge(S("log_f"), 1)
                dve.wait_ge(S("scan_loaded"), 16)
                for h in range(BH):
                    dve.tensor_tensor_scan(bcum[:, h, :], t3[:, 0:SEQ], qe[:, h, :], 0.0, ALU.mult, ALU.add).then_inc(S("cum_done"), 1)
                drain(19, 19)
                prefetch(n0 + 19)
                by_chunk = "p h (n t) -> p (h n) t"
                b4 = bcum[:].rearrange(by_chunk, t=CHUNK)
                dve.wait_ge(S("cum_done"), BH)
                dve.tensor_tensor(kd[:].rearrange(by_chunk, t=CHUNK),
                                  b4[:, :, CHUNK - 1:CHUNK].to_broadcast([P, BH * SEQ // CHUNK, CHUNK]), b4, ALU.subtract) \
                    .then_inc(S("to_end"), 1)
                drain(20, 20)
                prefetch(n0 + 20)
                dve.wait_ge(S("exp_cum"), 1)
                dve.tensor_copy(decay[:].rearrange("p h n -> p (h n)"), qe[:].rearrange(by_chunk, t=CHUNK)[:, :, CHUNK - 1]) \
                    .then_inc(S("gates_ready"), 1)
                dve.wait_ge(S("silus"), 1)
                dve.tensor_scalar(z[:, Z_Q:Z_Q + BH, SEQ:NT], z[:, Z_Q:Z_Q + BH, SEQ:NT], DK ** -0.5, None, ALU.mult) \
                    .then_inc(S("gates_ready"), 1)
                dve.wait_ge(S("gates_ready"), 2)
                dve.scalar_tensor_tensor(qe[:], z[:, Z_Q:Z_Q + BH, 0:SEQ], DK ** -0.5, qe[:], op0=ALU.mult, op1=ALU.mult) \
                    .then_inc(S("gates_ready"), 1)
                drain(21, 21)
                prefetch(n0 + 21)
                for n, t in enumerate((ke, kd)):
                    dve.wait_ge(S("exp_cum"), n + 2)
                    dve.wait_ge(S("k_all_ready"), 1)
                    dve.tensor_tensor(t[:], k_all[:, :, 0:SEQ], t[:], ALU.mult).then_inc(S("gates_ready"), 1)
                for c in range(QC):
                    dve.wait_ge(S("cq_hi_done"), c + 1)
                    dve.scalar_tensor_tensor(cq_lo[:, c, :], z[:, Z_CQ + c, :], gain[:, G_Q + c:G_Q + c + 1], cq_hi[:, c, :],
                                             op0=ALU.mult, op1=ALU.subtract).then_inc(S("cq_lo_done"), 1)
                pe_rows, sw_rows = slice(NOPE, NOPE + ROPE), slice(NOPE + ROPE, P)
                dve.wait_ge(S("drained"), 2 * (g0 + AB_UNITS))
                dve.tensor_tensor(t1[pe_rows, :], z[pe_rows, Z_KPE, :], cst[pe_rows, C_ROPE:C_ROPE + NT], ALU.mult).then_inc(S("k_pe_step"), 1)
                dve.tensor_tensor(t2[pe_rows, :], z[sw_rows, Z_KPE, :], cst[sw_rows, C_ROPE:C_ROPE + NT], ALU.mult).then_inc(S("k_pe_step"), 1)
                dve.wait_ge(S("k_pe_step"), 2)
                dve.tensor_tensor(k_pe[pe_rows, :], t1[pe_rows, :], t2[pe_rows, :], ALU.add).then_inc(S("k_pe_step"), 1)

            def hgrn():
                chunk_mask = cst[:, C_CHUNK:C_CHUNK + CH_BLK]
                intra = cst[:, C_INTRA:C_INTRA + P].bitcast(I32)

                def masked(m):
                    dve.wait_ge(S("kv_kept"), m + 1)
                    if m >= 2:
                        dve.wait_ge(S("o_mm"), m - 1)
                    dve.tensor_tensor(v_blk[m % 2][:], kdv[m % 2][:, 1:2, :].to_broadcast([P, CH_BLK, P]),
                                      chunk_mask.unsqueeze(2).to_broadcast([P, CH_BLK, P]), ALU.mult).then_inc(S("v_blocks"), 1)
                    dve.wait_ge(S("att_mm"), m + 1)
                    dve.wait_ge(S("att_zeroed"), 2)
                    dve.copy_predicated(att[m % 2][:], intra, bank[2 + m % 2][:, 0:P]).then_inc(S("att_masked"), 1)

                masked(0)
                for m in range(BH * BLOCKS):
                    h, b = divmod(m, BLOCKS)
                    dve.wait_ge(S("state_mm"), m + 1)
                    for c in range(CH_BLK):
                        e = CH_BLK * m + c
                        kv = bank[4 + c // 4][:, (c % 4) * P:(c % 4 + 1) * P]
                        to = s_ring[:, (e + 1) % (2 * CH_BLK), :]
                        if c == CH_BLK - 1 and m:
                            dve.wait_ge(S("o_mm"), m)
                        if b == 0 and c == 0:
                            dve.tensor_copy(to, kv).then_inc(S("state_step"), 1)
                        else:
                            dve.wait_ge(S("state_step"), e)
                            dve.scalar_tensor_tensor(to, s_ring[:, e % (2 * CH_BLK), :], decay[:, h, CH_BLK * b + c:CH_BLK * b + c + 1],
                                                     kv, op0=ALU.mult, op1=ALU.add).then_inc(S("state_step"), 1)
                    if b == BLOCKS - 1:
                        dve.wait_ge(S("state_step"), CH_BLK * (m + 1))
                        dve.tensor_copy(s_fin[:, h, :], s_ring[:, (CH_BLK * (m + 1)) % (2 * CH_BLK), :]).then_inc(S("final_kept"), 1)
                    if m == 0:
                        dve.wait_ge(S("factor"), factors_before(1) + 6)
                        for c in range(CC):
                            dve.scalar_tensor_tensor(ckv[:, c, :], z[:, Z_CKV + c, :], gain[:, G_KV + c:G_KV + c + 1], t3[:],
                                                     op0=ALU.mult, op1=ALU.mult).then_inc(S("ckv_ready"), 1)
                        dve.tensor_tensor(rope_r[NOPE:P, :], cst[NOPE:P, C_ROPE:C_ROPE + NT], r[NOPE:P, :], ALU.mult) \
                            .then_inc(S("rope_ready"), 1)
                    if m == 1:
                        dve.wait_ge(S("ckv_hi_done"), 1)
                        dve.wait_ge(S("ckv_ready"), CC)
                        dve.tensor_tensor(ckv_lo[:], ckv[:], ckv_hi[:], ALU.subtract).then_inc(S("ckv_lo_done"), 1)
                    if m + 1 < BH * BLOCKS:
                        masked(m + 1)
                v_s = z[:, Z_I:Z_I + BH, SEQ:NT]
                for b in range(BATCH_D):
                    if b == 0:
                        dve.wait_ge(S("cq_summed"), 4)
                    else:
                        dve.wait_ge(S("v_spread"), b)
                    dve.tensor_tensor(v_diag[:], ident.unsqueeze(1).to_broadcast([P, BH, P]),
                                      v_s[:, :, b:b + 1].to_broadcast([P, BH, P]), ALU.mult).then_inc(S("v_diag_ready"), 1)
                    dve.wait_ge(S(f"st_loaded{b % 2}"), 16 * (b // 2 + 1))
                    dve.tensor_tensor(st[b % 2][:], st[b % 2][:], z[:, Z_F:Z_F + BH, SEQ + b:SEQ + b + 1].to_broadcast([P, BH, P]),
                                      ALU.mult).then_inc(S("s_decayed"), 1)
                    dve.wait_ge(S("v_spread"), b + 1)
                    if b:
                        dve.wait_ge(S("s_new"), b)
                    dve.tensor_tensor(s_tmp[:], bank[4 + b % 2][:].rearrange("p (h d) -> p h d", h=BH),
                                      k_all[:, :, SEQ + b:SEQ + b + 1].to_broadcast([P, BH, P]), ALU.mult).then_inc(S("kv_made"), 1)
                    dve.wait_ge(S("kv_made"), b + 1)
                    dve.tensor_tensor(st[b % 2][:], st[b % 2][:], s_tmp[:], ALU.add).then_inc(S("s_new"), 1)
                dve.wait_ge(S("os_mm"), BATCH_D)
                dve.tensor_copy(z[:, Z_Q:Z_Q + BH, SEQ:NT], bank[6][:, 0:BH * BATCH_D].rearrange("p (h b) -> p h b", h=BH)) \
                    .then_inc(S("os_kept"), 1)
                o_all = z[:, Z_Q:Z_Q + BH, :]
                dve.wait_ge(S("o_factor"), 1)
                dve.scalar_tensor_tensor(o_all, o_all, gain[:, G_OUT:G_OUT + 1], o_fac[:], op0=ALU.mult, op1=ALU.mult).then_inc(S("o_step"), 1)
                dve.wait_ge(S("o_step"), 1)
                dve.tensor_tensor(o_all, o_all, z[:, Z_G:Z_G + BH, :], ALU.mult).then_inc(S("o_step"), 1)
                dve.wait_ge(S("mix_hi_done"), 1)
                dve.wait_ge(S("o_step"), 2)
                dve.tensor_tensor(m_lo[:, BH:, :], o_all, m_hi[:, BH:, :], ALU.subtract).then_inc(S("mix_lo_done"), 1)

            def qkv():
                n0, g0 = U0["uq"], G0["uq"]
                pe_rows, sw_rows = slice(NOPE, NOPE + ROPE), slice(NOPE + ROPE, P)
                dve.wait_ge(S("mix_lo_done"), 1)
                dve.wait_ge(S("s_fin_stored"), 16)
                dve.wait_ge(S("rope_ready"), 1)
                for h in range(HEADS):
                    for hf in range(2):
                        ps = pair(g0 + h, hf)
                        if h < HEADS - 1:
                            dve.wait_ge(S("q_mm"), 2 * h + hf + 1)
                        else:
                            dve.wait_ge(S("half_done"), 2 * (n0 + 2) + hf + 1)
                        if 2 * h + hf >= 2:
                            dve.wait_ge(S("q_ready"), 2 * h + hf - 1)
                        dve.tensor_tensor(q_t[0:NOPE, h, half[hf]], ps[0:NOPE, :], r[0:NOPE, half[hf]], ALU.mult).then_inc(S("q_part"), 1)
                        dve.tensor_tensor(t1[pe_rows, half[hf]], ps[pe_rows, :], rope_r[pe_rows, half[hf]], ALU.mult).then_inc(S("q_part"), 1)
                        dve.tensor_tensor(t2[pe_rows, half[hf]], ps[sw_rows, :], rope_r[sw_rows, half[hf]], ALU.mult).then_inc(S("drained"), 1)
                        dve.wait_ge(S("drained"), 2 * (g0 + h) + hf + 1)
                        dve.tensor_tensor(q_t[pe_rows, h, half[hf]], t1[pe_rows, half[hf]], t2[pe_rows, half[hf]], ALU.add) \
                            .then_inc(S("q_ready"), 1)
                    if h in (2, 5, 7):
                        prefetch(n0 + (2, 5, 7).index(h))
                for t in range(BLOCKS):
                    if t < BLOCKS - 1:
                        dve.wait_ge(S("v_mm"), t + 1)
                    else:
                        dve.wait_ge(S("half_done"), 2 * (U0["ukv"] + UKV_UNITS))
                    dve.tensor_copy(v_t[:, t, :], bank[4 + t][:]).then_inc(S("v_kept"), 1)
                for u in range(UKV_UNITS):
                    prefetch(U0["ukv"] + u)

            def attention():
                dve.wait_ge(S("att_cleared"), 2)
                dve.wait_ge(S("q_lat_mm"), 1)
                dve.tensor_copy(q_lat[:].rearrange("p b c h -> p c h b"),
                                bank[1][:, 0:CC * HEADS * BATCH_D].rearrange("p (c h b) -> p c h b", c=CC, h=HEADS)) \
                    .then_inc(S("q_s_ready"), 1)
                for j in range(GRP):
                    dve.tensor_copy(q_pe4[ROPE * j:ROPE * (j + 1), :, HEADS * j:HEADS * (j + 1)].rearrange("p b h -> p h b"),
                                    q_t[NOPE:NOPE + ROPE, :, SEQ:NT]).then_inc(S("q_s_ready"), 1)
                causal = cst[:, C_CAUSAL:C_CAUSAL + P]
                for i in range(HEADS):
                    dve.wait_ge(S("s_mm"), i + 1)
                    for b in range(BLOCKS):
                        s = score_at[b]
                        dve.tensor_tensor(s[:, b * P:(b + 1) * P], s[:, b * P:(b + 1) * P], causal, ALU.add).then_inc(S("s_masked"), 1)
                        dve.wait_ge(S("s_masked"), BLOCKS * i + b + 1)
                        dve.reduce_max(mx_p[:, 0, b:b + 1], s, AX.X).then_inc(S("max_taken"), 1)
                    dve.wait_ge(S("max_taken"), BLOCKS * (i + 1))
                    if i:
                        dve.wait_ge(S("p_exp"), BLOCKS * i)
                    dve.tensor_scalar(mx_p[:, 1, :], mx_p[:, 0, :], -SM_SCALE, None, ALU.mult).then_inc(S("max_scaled"), 1)
                    dve.wait_ge(S("p_exp"), BLOCKS * (i + 1))
                    dve.reciprocal(sum_p[:, 1, :], sum_p[:, 0, :]).then_inc(S("sum_inverse"), 1)
                    dve.wait_ge(S("sum_inverse"), i + 1)
                    for b in range(BLOCKS):
                        p = prob[:, tri(b):tri(b + 1), :]
                        dve.tensor_scalar(p, p, sum_p[:, 1, b:b + 1], None, ALU.mult).then_inc(S("p_ready"), 1)
                    dve.wait_ge(S("sc_mm"), i + 1)
                    if i:
                        dve.wait_ge(S("pr_exp"), i)
                    dve.tensor_copy(sc[:, 0:PAGES, :].rearrange("p g h -> p (g h)"), bank[0][:, 0:PAGES * HEADS]).then_inc(S("sc_kept"), 1)
                    dve.tensor_copy(sc[0:1, PAGES, :], bank[0][0:1, PAGES * HEADS:(PAGES + 1) * HEADS]).then_inc(S("sc_kept"), 1)
                    dve.wait_ge(S("sc_kept"), 2 * i + 2)
                    mx, row, dg, sm, inv = (small[:, k, :] for k in range(5))
                    dve.reduce_max(mx, sc[:].rearrange("p g h -> p h g"), AX.X).then_inc(S("mx_taken"), 1)
                    dve.wait_ge(S("mx_turned"), i + 1)
                    dve.reduce_max(row[0:HEADS, 0:1], bank[0][0:HEADS, 384:512], AX.X).then_inc(S("mx_row"), 1)
                    dve.wait_ge(S("mx_row"), i + 1)
                    dve.tensor_scalar(dg[0:HEADS, :], ident[0:HEADS, 0:HEADS], row[0:HEADS, 0:1], None, ALU.mult).then_inc(S("mx_diag"), 1)
                    dve.wait_ge(S("mx_spread"), i + 1)
                    dve.tensor_tensor(sc[:], sc[:], bank[0][:, 264:272].unsqueeze(1).to_broadcast([P, PAGES + 1, HEADS]), ALU.subtract) \
                        .then_inc(S("sc_shifted"), 1)
                    dve.wait_ge(S("pr_exp"), i + 1)
                    dve.reduce_sum(sm, pr[:].rearrange("p g h -> p h g"), AX.X).then_inc(S("sum_taken"), 1)
                    rows = slice(i % 2 * VDIM, (i % 2 + 1) * VDIM)
                    dve.wait_ge(S("oa_hi_done"), i + 1)
                    dve.tensor_tensor(m_lo[rows, i // 2, 0:SEQ], bank[4][rows, :], m_hi[rows, i // 2, 0:SEQ], ALU.subtract) \
                        .then_inc(S("oa_lo_done"), 1)
                    dve.wait_ge(S("sum_spread"), i + 1)
                    dve.reciprocal(inv, bank[0][:, 272:280]).then_inc(S("pr_inverse"), 1)
                    dve.wait_ge(S("pr_inverse"), i + 1)
                    dve.wait_ge(S("pv_mm"), i + 1)
                    for c in range(CC):
                        dve.tensor_tensor(o_lat[:, c, :, i], bank[2 + c][:, 0:HEADS], inv, ALU.mult).then_inc(S("o_lat_ready"), 1)
                for i in range(HEADS):
                    rows = slice(i % 2 * VDIM, (i % 2 + 1) * VDIM)
                    dve.wait_ge(S("oa_hi_done"), 2 * HEADS)
                    dve.tensor_tensor(m_lo[rows, i // 2, SEQ:NT], bank[0][rows, i * BATCH_D:(i + 1) * BATCH_D],
                                      m_hi[rows, i // 2, SEQ:NT], ALU.subtract).then_inc(S("oa_lo_done"), 1)

            def conv():
                n0, g0 = U0["c"], G0["c"]
                dve.wait_ge(S("drained"), 2 * g0)
                dve.memset(v_ext[:, 0:2], 0.0).then_inc(S("v_padded"), 1)

                def chunk(j0, count, i):
                    st = None if isinstance(i, int) else Step(i, 3)
                    j = j0
                    jj = j if st is None else j + i
                    n, g = n0 + 3 * j, g0 + 3 * j
                    nn, gg = n0 + 3 * jj, g0 + 3 * jj
                    tap = [gain[:, bass.ds(G_CONV + KC * k + jj, 1)] for k in range(3)]
                    if st is None:
                        factor_ready(READS["c"])
                        dve.wait_ge(S("v_padded"), 1)

                    def drain(u, to):
                        for hf in range(2):
                            dve.wait_ge(S("half_done"), 2 * (nn + u) + hf + 1)
                            dve.tensor_tensor(to[:, half[hf]], pair(g + u, hf), r[:, half[hf]], ALU.mult).then_inc(S("drained"), 1)

                    if st is not None:
                        dve.wait_ge(S("mix_lo_done"), jj + 1)
                    drain(0, t1)
                    prefetch(n, st)
                    drain(1, t3)
                    dve.wait_ge(S("drained"), 2 * (gg + 2))
                    if st is not None:
                        dve.wait_ge(S("conv_kept"), 2 * jj)
                    for hf in range(2):
                        dve.tensor_tensor(v_ext[:, 2 + hf * HALF:2 + (hf + 1) * HALF], t1[:, half[hf]], t3[:, half[hf]], ALU.mult) \
                            .then_inc(S("v_ready"), 1)
                    prefetch(n + 1, st)
                    dve.wait_ge(S("v_ready"), 2 * jj + 2)
                    if st is None:
                        dve.wait_ge(S("conv_st_loaded"), 16)
                    y, y_s = t2[:, 0:SEQ], t2[:, SEQ:NT]
                    dve.tensor_scalar(y, v_ext[:, 0:SEQ], tap[0], None, ALU.mult).then_inc(S("tap_done"), 1)
                    dve.tensor_scalar(y_s, conv_st[:, jj, 0, :], tap[0], None, ALU.mult).then_inc(S("tap_done"), 1)
                    dve.wait_ge(S("tap_done"), 6 * jj + 2)
                    dve.scalar_tensor_tensor(y, v_ext[:, 1:1 + SEQ], tap[1], y, op0=ALU.mult, op1=ALU.add).then_inc(S("tap_done"), 1)
                    dve.scalar_tensor_tensor(y_s, conv_st[:, jj, 1, :], tap[1], y_s, op0=ALU.mult, op1=ALU.add).then_inc(S("tap_done"), 1)
                    dve.wait_ge(S("tap_done"), 6 * jj + 4)
                    dve.scalar_tensor_tensor(y, v_ext[:, 2:2 + SEQ], tap[2], y, op0=ALU.mult, op1=ALU.add).then_inc(S("tap_done"), 1)
                    dve.scalar_tensor_tensor(y_s, v_ext[:, 2 + SEQ:2 + NT], tap[2], y_s, op0=ALU.mult, op1=ALU.add).then_inc(S("tap_done"), 1)
                    dve.wait_ge(S("tap_done"), 6 * jj + 6)
                    drain(2, t3)
                    dve.wait_ge(S("drained"), 2 * (gg + 3))
                    dve.tensor_tensor(t1[:], t3[:], t2[:], ALU.mult).then_inc(S("c_gated"), 1)
                    prefetch(n + 2, st)
                    dve.wait_ge(S("mix_hi_done"), jj + 2)
                    dve.tensor_tensor(m_lo[:, jj, :], t1[:], m_hi[:, jj, :], ALU.subtract).then_inc(S("mix_lo_done"), 1)

                over(dve, C_PEEL, KC, 1, chunk)

            dve.wait_ge(S("x_loaded"), 16)
            dve.wait_ge(S("gain_loaded"), 16)
            logit = [gain[:, G_LB + BH * k:G_LB + BH * (k + 1)] for k in range(3)]
            dve.tensor_tensor(lb[:, 3, :], logit[0], logit[1], ALU.max).then_inc(S("lb_max"), 1)
            dve.wait_ge(S("lb_max"), 1)
            dve.tensor_tensor(lb[:, 3, :], lb[:, 3, :], logit[2], ALU.max).then_inc(S("lb_max"), 1)
            dve.wait_ge(S("lb_max"), 2)
            for k in range(3):
                dve.tensor_tensor(lb[:, k, :], logit[k], lb[:, 3, :], ALU.subtract).then_inc(S("lb_step"), 1)
            for d in range(KC):
                chunk_dve(0, d, d)
            for n in range(3):
                split_lo(n)
            dve.wait_ge(S("lb_exp"), 1)
            dve.tensor_tensor(lb[:, 3, :], lb[:, 0, :], lb[:, 1, :], ALU.add).then_inc(S("lb_step"), 1)
            dve.wait_ge(S("lb_step"), 4)
            dve.tensor_tensor(lb[:, 3, :], lb[:, 3, :], lb[:, 2, :], ALU.add).then_inc(S("lb_step"), 1)
            dve.wait_ge(S("lb_step"), 5)
            dve.reciprocal(lb[:, 3, :], lb[:, 3, :]).then_inc(S("lb_step"), 1)
            dve.wait_ge(S("lb_step"), 6)
            dve.tensor_tensor(lb[:, 2, :], lb[:, 0, :], lb[:, 3, :], ALU.mult).then_inc(S("lb_step"), 1)
            dve.wait_ge(S("lb_step"), 7)
            dve.tensor_scalar(lb[:, 3, :], lb[:, 2, :], -1.0, 1.0, ALU.mult, ALU.add).then_inc(S("lb_step"), 1)
            dve.wait_ge(S("lb_step"), 8)
            ffn("ffn0")
            ab_in()
            hgrn()
            qkv()
            attention()
            out_projection("ab_out", 2)
            ffn("ffn1")
            ffn("ffn2")
            conv()
            out_projection("c_out", 5)
            ffn("ffn3")
            factor_ready(6)
            dve.wait_ge(S("x_added"), 2 * 6 * KC)
            for d in range(KC):
                dve.scalar_tensor_tensor(x[:, d, :], x[:, d, :], gain[:, G_FINAL + d:G_FINAL + d + 1], r[:], op0=ALU.mult, op1=ALU.mult) \
                    .then_inc(S("y_ready"), 1)

        @block.tensor
        def _(pe):
            mm = nc.tensor.matmul

            def stream_ready(res):
                def wait_chunk(c, hf):
                    pe.wait_ge(S("h_lo_done"), 16 * res + 2 * c + hf + 1)
                return wait_chunk

            def ffn(name):
                n0, g0, res, no = U0[name], G0[name], READS[name], FFN_NO[name]

                def gate_up(f0, count, i):
                    st = None if isinstance(i, int) else Step(i, 2 * count)
                    for f in range(f0, f0 + count):
                        ff = f if st is None else f + i * count
                        for u in range(2):
                            first = st is None and f == 0 and u == 0
                            if g0 + 2 * f + u >= 3:
                                group_free(g0 + 2 * ff + u)
                            unit_ready(n0 + 2 * ff + u)
                            multiply((n0 + 2 * f + u) % 3, g0 + 2 * f + u, h_hi, h_lo, 0, KC, True, True,
                                     stream_ready(res) if first else None)
                            if first:
                                norm_sum(res)

                over(pe, GATE_PEEL, FC, 3, gate_up)
                n0 += GATE_UNITS
                g0 += GATE_UNITS

                def down(d0, count, i):
                    st = None if isinstance(i, int) else Step(i, 3 * count)
                    for d in range(d0, d0 + count):
                        dd = d if st is None else d + i * count
                        group_free(g0 + dd)
                        for u in range(DOWN_U):
                            unit_ready(n0 + 3 * dd + u)
                            if st is None and d == 0 and u == 0:
                                pe.wait_ge(S("a_lo_done"), (no + 1) * 2 * FC - 2)
                            if st is None and d == 0 and u == 2:
                                pe.wait_ge(S("a_lo_done"), (no + 1) * 2 * FC)
                            multiply((n0 + 3 * d + u) % 3, g0 + d, a_hi, a_lo, 8 * u, min(8, FC - 8 * u), u == 0, u == 2)

                over(pe, OUT_PEEL, KC, 3, down, tail(name))

            def in_columns(name, count_units, peel, per):
                n0, g0, res = U0[name], G0[name], READS[name]

                def column(u0, count, i):
                    st = None if isinstance(i, int) else Step(i, count)
                    for u in range(u0, u0 + count):
                        uu = u if st is None else u + i * count
                        group_free(g0 + uu)
                        unit_ready(n0 + uu)
                        first = st is None and u == 0
                        multiply((n0 + u) % 3, g0 + u, h_hi, h_lo, 0, KC, True, True, stream_ready(res) if first else None)
                        if first:
                            norm_sum(res)

                over(pe, peel, count_units, per, column)

            def out_projection(name, mixed):
                n0, g0 = U0[name], G0[name]

                def column(d0, count, i):
                    st = None if isinstance(i, int) else Step(i, count)
                    for d in range(d0, d0 + count):
                        dd = d if st is None else d + i * count
                        group_free(g0 + dd)
                        unit_ready(n0 + dd)
                        multiply((n0 + d) % 3, g0 + d, m_hi, m_lo, 0, KC, True, True,
                                 mixed if st is None and d == 0 else None)

                over(pe, OUT_PEEL, KC, 3, column)

            def ab_in():
                in_columns("ab", AB_UNITS, Z_PEEL, 3)
                g0 = G0["ab"]
                for k, chunks in enumerate((range(QC), range(QC, QC + CC))):
                    pe.wait_ge(S("c_squared"), chunks[-1] + 1)
                    if k == 1:
                        pe.wait_ge(S("log_taken"), factors_before(1) + 4)
                    for hf in range(2):
                        for c in chunks:
                            sq = squares[:, c, half[hf]] if c < 4 else acc[:, half[hf]]
                            last = mm(bank[6 + hf][:, 0:HALF], ones, sq, start=c == chunks[0], stop=c == chunks[-1])
                        last.then_inc(S("cq_summed"), 1)

            def hgrn():
                g0 = G0["ab"]

                def scores(m):
                    h, b = divmod(m, BLOCKS)
                    if m >= 2:
                        pe.wait_ge(S("kv_kept"), m - 1)
                        pe.wait_ge(S("att_masked"), m - 1)
                    nc.tensor.transpose(bank[m % 2][:, 0:P], kd[:, h, o_block(h, b)], ident)
                    nc.tensor.transpose(bank[m % 2][:, P:2 * P], z[:, Z_I + h, o_block(h, b)], ident).then_inc(S("kv_transposed"), 1)
                    mm(bank[2 + m % 2][:, 0:P], ke[:, h, o_block(h, b)], qe[:, h, o_block(h, b)], start=True, stop=True) \
                        .then_inc(S("att_mm"), 1)

                pe.wait_ge(S("drained"), 2 * (g0 + AB_UNITS))
                pe.wait_ge(S("gates_ready"), 5)
                scores(0)
                for m in range(BH * BLOCKS):
                    h, b = divmod(m, BLOCKS)
                    pe.wait_ge(S("v_blocks"), m + 1)
                    if m:
                        pe.wait_ge(S("state_step"), CH_BLK * m)
                    for k in range(2):
                        last = mm(bank[4 + k][:], kdv[m % 2][:, 0, :], v_blk[m % 2][:, 4 * k:4 * k + 4, :], start=True, stop=True)
                    last.then_inc(S("state_mm"), 1)
                    if m + 1 < BH * BLOCKS:
                        scores(m + 1)
                    pe.wait_ge(S("att_masked"), m + 1)
                    if m == 0:
                        pe.wait_ge(S("factor"), factors_before(1) + 6)
                    if m >= 2:
                        pe.wait_ge(S("o_kept"), m - 1)
                    out = bank[6 + m % 2][:, 0:P]
                    mm(out, kdv[m % 2][:, 1, :], att[m % 2][:], start=True, stop=False)
                    for c in range(1 if b == 0 else 0, CH_BLK):
                        e = CH_BLK * m + c
                        if e:
                            pe.wait_ge(S("state_step"), e)
                        cols = slice(b * P + c * CHUNK, b * P + (c + 1) * CHUNK)
                        last = mm(out[:, c * CHUNK:(c + 1) * CHUNK], s_ring[:, e % (2 * CH_BLK), :], qe[:, h, cols],
                                  start=False, stop=c == CH_BLK - 1)
                    last.then_inc(S("o_mm"), 1)
                pe.wait_ge(S("state_step"), CH_BLK * BH * BLOCKS)
                pe.wait_ge(S("o_kept"), BH * BLOCKS)
                for b in range(BATCH_D):
                    pe.wait_ge(S("v_diag_ready"), b + 1)
                    if b >= 2:
                        pe.wait_ge(S("kv_made"), b - 1)
                    mm(bank[4 + b % 2][:], ones, v_diag[:], start=True, stop=True).then_inc(S("v_spread"), 1)
                    pe.wait_ge(S("s_new"), b + 1)
                    for h in range(BH):
                        at_o = h * BATCH_D + b
                        last = mm(bank[6][:, at_o:at_o + 1], st[b % 2][:, h, :], z[:, Z_Q + h, SEQ + b:SEQ + b + 1], start=True, stop=True)
                    last.then_inc(S("os_mm"), 1)
                pe.wait_ge(S("o_squared"), 1)
                for h in range(BH):
                    for hf in range(2):
                        mm(bank[2 * h + hf][:, 0:HALF], ones, k_all[:, h, half[hf]], start=True, stop=True).then_inc(S("o_summed"), 1)

            def qkv():
                n0, g0 = U0["uq"], G0["uq"]
                pe.wait_ge(S("cq_lo_done"), QC)
                pe.wait_ge(S("o_log"), 2 * BH)
                for h in range(HEADS):
                    if h >= 3:
                        group_free(g0 + h)
                    unit_ready(n0 + (QC * h + QC - 1) // 8)
                    for hf in range(2):
                        out = pair(g0 + h, hf)
                        for c in range(QC):
                            u, t = divmod(QC * h + c, 8)
                            wh, wl = w_hi[(n0 + u) % 3][:, t, :], w_lo[(n0 + u) % 3][:, t, :]
                            xh, xl = cq_hi[:, c, half[hf]], cq_lo[:, c, half[hf]]
                            mm(out, wh, xh, start=c == 0, stop=False)
                            mm(out, wh, xl, start=False, stop=False)
                            last = mm(out, wl, xh, start=False, stop=c == QC - 1)
                            if t == 7:
                                last.then_inc(S("half_done"), 1)
                        if h < HEADS - 1:
                            last.then_inc(S("q_mm"), 1)
                n0 = U0["ukv"]
                unit_ready(n0 + UKV_UNITS - 1)
                pe.wait_ge(S("ckv_lo_done"), 1)
                w = [(w_hi[(n0 + c) % 3], w_lo[(n0 + c) % 3]) for c in range(CC)]
                pe.wait_ge(S("drained"), 2 * (g0 + HEADS))
                for h in range(HEADS):
                    if h >= 4:
                        pe.wait_ge(S("k_kept"), HEADS + h - 3)
                    for c in range(CC):
                        out, xh, xl = bank[h % 4][:], ckv_hi[:, c, 0:SEQ], ckv_lo[:, c, 0:SEQ]
                        mm(out, w[c][0][:, h, :], xh, start=c == 0, stop=False)
                        mm(out, w[c][0][:, h, :], xl, start=False, stop=False)
                        last = mm(out, w[c][1][:, h, :], xh, start=False, stop=c == CC - 1)
                    last.then_inc(S("k_done"), 1)
                for t in range(BLOCKS):
                    tok = slice(t * P, (t + 1) * P)
                    for c in range(CC):
                        out, xh, xl = bank[4 + t][:], ckv_hi[:, c, tok], ckv_lo[:, c, tok]
                        wh, wl = (w[c][k][:, :, NOPE:NOPE + VDIM] for k in range(2))
                        mm(out, xh, wh, start=c == 0, stop=False)
                        one = mm(out, xl, wh, start=False, stop=False)
                        last = mm(out, xh, wl, start=False, stop=c == CC - 1)
                        if t == BLOCKS - 1:
                            one.then_inc(S("half_done"), 1)
                            last.then_inc(S("half_done"), 1)
                    if t < BLOCKS - 1:
                        last.then_inc(S("v_mm"), 1)

            def attention():
                pe.wait_ge(S("w_uk_loaded"), 16)
                pe.wait_ge(S("k_kept"), 2 * HEADS)
                pe.wait_ge(S("q_ready"), 2 * HEADS)
                for c in range(CC):
                    for h in range(HEADS):
                        at_q = (c * HEADS + h) * BATCH_D
                        last = mm(bank[1][:, at_q:at_q + BATCH_D], w_uk[:, h, c * P:(c + 1) * P], q_t[0:NOPE, h, SEQ:NT],
                                  start=True, stop=True)
                last.then_inc(S("q_lat_mm"), 1)
                pe.wait_ge(S("v_kept"), BLOCKS)
                groups = PAGES // GRP
                for i in range(HEADS):
                    if i:
                        pe.wait_ge(S("pt_kept"), 3 * i)
                    for b in range(BLOCKS):
                        last = mm(score_at[b], q_t[0:NOPE + ROPE, i, b * P:(b + 1) * P], k_t[0:NOPE + ROPE, i, 0:(b + 1) * P],
                                  start=True, stop=True)
                    last.then_inc(S("s_mm"), 1)

                    def turn_keys(g):
                        n = i * groups + g
                        pe.wait_ge(S("kp_gathered"), n + 1)
                        if n:
                            pe.wait_ge(S("kp_kept"), n)
                        else:
                            pe.wait_ge(S("q_s_ready"), 1)
                        nc.tensor.transpose(bank[1][:, (n % 2) * P:(n % 2 + 1) * P], kc[n % 2][:].rearrange("p j r -> p (j r)"), ident) \
                            .then_inc(S("kp_transposed"), 1)

                    turn_keys(0)
                    pe.wait_ge(S("q_s_ready"), 1 + GRP)
                    if i:
                        pe.wait_ge(S("pr_inverse"), i)
                    for g in range(groups):
                        n = i * groups + g
                        slot = lat_t[n % T_SLOTS]
                        pe.wait_ge(S("kp_kept"), n + 1)
                        if g + 1 < groups:
                            turn_keys(g + 1)
                        mm(bank[0][:, GRP * HEADS * g:GRP * HEADS * (g + 1)], kp[n % 2][:], q_pe4[:, i, :], start=True, stop=False)
                        for j in range(GRP):
                            at_s = (GRP * g + j) * HEADS
                            for c in range(CC):
                                last = mm(bank[0][:, at_s:at_s + HEADS], slot[:, j, c * P:(c + 1) * P], q_lat[:, i, c, :],
                                          start=False, stop=j == GRP - 1 and c == CC - 1)
                        last.then_inc(S("lat_t_used"), 1)
                    own = bank[0][0:1, PAGES * HEADS:(PAGES + 1) * HEADS]
                    for c in range(CC):
                        mm(own, ckv[:, c, SEQ + i:SEQ + i + 1], q_lat[:, i, c, :], start=c == 0, stop=False)
                    mm(own, q_key[:, i:i + 1], q_own[:, i, :], start=False, stop=True).then_inc(S("sc_mm"), 1)
                    for c in range(CC):
                        last = nc.tensor.transpose(bank[1][0:1, (2 + c) * P:(3 + c) * P], ckv[:, c, SEQ + i:SEQ + i + 1], ident)
                    last.then_inc(S("self_transposed"), 1)
                    pe.wait_ge(S("p_ready"), BLOCKS * (i + 1))
                    for e in range(10):
                        last = nc.tensor.transpose(bank[5 + e // 4][:, (e % 4) * P:(e % 4 + 1) * P], prob[:, e, :], ident)
                        if e in (3, 7, 9):
                            last.then_inc(S("p_transposed"), 1)
                    pe.wait_ge(S("mx_taken"), i + 1)
                    nc.tensor.transpose(bank[0][0:HEADS, 384:512], small[:, 0, :], ident).then_inc(S("mx_turned"), 1)
                    pe.wait_ge(S("pt_kept"), 3 * (i + 1))
                    if i:
                        pe.wait_ge(S("oa_lo_done"), i)
                    vals = slice(i // 2 * P, (i // 2 + 1) * P)
                    for b in range(BLOCKS):
                        for k in range(b + 1):
                            last = mm(bank[4][:, b * P:(b + 1) * P], v_t[:, k, vals], prob_t[:, tri(b) + k, :], start=k == 0, stop=k == b)
                    last.then_inc(S("o_a_mm"), 1)
                    pe.wait_ge(S("mx_diag"), i + 1)
                    mm(bank[0][:, 264:272], ones[0:HEADS, :], small[0:HEADS, 2, :], start=True, stop=True).then_inc(S("mx_spread"), 1)
                    pe.wait_ge(S("pr_exp"), i + 1)
                    pe.wait_ge(S("self_kept"), i + 1)
                    if i:
                        pe.wait_ge(S("o_lat_ready"), 2 * i)
                    for g in range(groups):
                        n = i * groups + g
                        for j in range(GRP):
                            pe.wait_ge(S(f"lat_loaded{n % N_SLOTS}_{j}"), 16 * (n // N_SLOTS + 1))
                            for c in range(CC):
                                last = mm(bank[2 + c][:, 0:HEADS], lat[n % N_SLOTS][:, j, c * P:(c + 1) * P], pr[:, GRP * g + j, :],
                                          start=g == 0 and j == 0, stop=False)
                        last.then_inc(S("lat_used"), 1)
                    for c in range(CC):
                        last = mm(bank[2 + c][:, 0:HEADS], self_row[0:1, c * P:(c + 1) * P], pr[0:1, PAGES, :], start=False, stop=True)
                    last.then_inc(S("pv_mm"), 1)
                    pe.wait_ge(S("sum_taken"), i + 1)
                    mm(bank[0][:, 272:280], ones, small[:, 3, :], start=True, stop=True).then_inc(S("sum_spread"), 1)
                pe.wait_ge(S("w_uv_loaded"), 16)
                pe.wait_ge(S("o_lat_ready"), CC * HEADS)
                for i in range(HEADS):
                    pr_heads = slice(i // 2 * 2, i // 2 * 2 + 2)
                    for c in range(CC):
                        last = mm(bank[0][:, i * BATCH_D:(i + 1) * BATCH_D], w_uv[:, c, pr_heads, :].rearrange("p h v -> p (h v)"),
                                  o_lat[:, c, i, :], start=c == 0, stop=c == CC - 1)
                last.then_inc(S("os_a_mm"), 1)

            q_key, q_own = k_pe[NOPE:NOPE + ROPE, SEQ:NT], q_t[NOPE:NOPE + ROPE, :, SEQ:NT].rearrange("p h b -> p b h")

            def ab_mixed(c, hf):
                if c == 0 and hf == 0:
                    pe.wait_ge(S("mix_lo_done"), 1)
                    pe.wait_ge(S("oa_lo_done"), 2 * HEADS)

            def c_mixed(c, hf):
                pe.wait_ge(S("mix_lo_done"), c + 2)

            pe.wait_ge(S("cst_loaded"), 16)
            ffn("ffn0")
            ab_in()
            hgrn()
            qkv()
            attention()
            out_projection("ab_out", ab_mixed)
            ffn("ffn1")
            ffn("ffn2")
            in_columns("c", C_UNITS, 3, 3)
            out_projection("c_out", c_mixed)
            ffn("ffn3")
            norm_sum(6)


def units(w):
    k, m = w.shape
    n = -(-k // (8 * P))
    full = np.zeros((n * 8 * P, m), w.dtype)
    full[:k] = w
    return full.reshape(n, 8, P, m // P, P).transpose(3, 0, 2, 1, 4).reshape(-1, P, UNIT)


def by_chunk(v):
    v = np.asarray(v)
    return np.moveaxis(v.reshape(v.shape[:-1] + (-1, P)), -1, 0)


def ffn_units(i, l, s):
    gate, up = (units(i[n][l, s]) for n in ("w_ffn_gate", "w_ffn_up"))
    both = np.stack([gate, up], axis=1).reshape(-1, P, UNIT)
    return [both, units(i["w_ffn_down"][l, s])]


def rope_columns(w):
    out = np.zeros((w.shape[0], P), w.dtype)
    out[:, 64:96] = w
    out[:, 96:128] = np.roll(w, ROPE // 2, axis=1)
    return out


def lay_out(i):
    w_in = i["w_in_ab"][0]
    cuts = np.cumsum([Q_LORA, KV_LORA, ROPE, BH * DK, BH * DK, BH * DK])
    c_q, c_kv, k_pe, q_b, f_b, i_b, g_b = np.split(w_in, cuts, axis=1)
    uq = i["w_uq"][0].reshape(Q_LORA, HEADS, NOPE + ROPE)
    uq = np.concatenate([uq, np.roll(uq[:, :, NOPE:], ROPE // 2, axis=2)], axis=2)
    uq = uq.reshape(QC, P, HEADS, P).transpose(2, 0, 1, 3).reshape(UQ_UNITS, 8, P, P).transpose(0, 2, 1, 3).reshape(UQ_UNITS, P, UNIT)
    ukv = i["w_ukv"][0].reshape(CC, P, UNIT)
    c_in = i["w_in_c"][0].reshape(D_MODEL, 3, D_MODEL)
    bg, cg, u = (units(c_in[:, k]) for k in range(3))
    c_in = np.stack([cg, u, bg], axis=1).reshape(-1, P, UNIT)
    stream = (ffn_units(i, 0, 0) + [units(t) for t in (q_b, g_b, f_b, i_b, c_q, c_kv, rope_columns(k_pe))] + [uq, ukv]
              + [units(i["w_out_ab"][0])] + ffn_units(i, 0, 1) + ffn_units(i, 1, 0) + [c_in, units(i["w_out_c"][0])]
              + ffn_units(i, 1, 1))
    w = np.concatenate(stream)
    assert w.shape[0] == N_UNITS
    gain = np.zeros((P, G_W), np.float32)
    gain[:, G_NORM:G_NORM + 48] = by_chunk(i["norm_g"]).reshape(P, 48)
    gain[:, G_FINAL:G_FINAL + KC] = by_chunk(i["final_norm_g"])
    gain[:, G_Q:G_Q + QC] = by_chunk(i["g_q_lora"][0])
    gain[:, G_KV:G_KV + CC] = by_chunk(i["g_kv_lora"][0])
    gain[:, G_LB:G_LB + 3 * BH] = by_chunk(i["hgrn_lower_bound"]).reshape(P, 3 * BH)
    gain[:, G_OUT:G_OUT + 1] = by_chunk(i["g_hgrn_out"][0])
    gain[:, G_CONV:G_CONV + 3 * KC] = by_chunk(i["w_conv_c"][0]).reshape(P, 3 * KC)
    cst = np.zeros((P, C_W), np.float32)
    cst[:, C_IDENT:C_IDENT + P] = np.eye(P)
    cst[:, C_ONES:C_ONES + P] = 1
    pos = np.concatenate([np.arange(SEQ), np.full(BATCH_D, PAGE * PAGES)]).astype(np.float32)
    inv = np.power(np.float32(10000.0), -np.arange(0, ROPE, 2, dtype=np.float32) / np.float32(ROPE)).astype(np.float32)
    ang = (inv[:, None] * pos[None, :]).astype(np.float32)
    cos, sin = np.cos(ang), np.sin(ang)
    cst[64:96, C_ROPE:C_ROPE + NT] = np.concatenate([cos, cos])
    cst[96:128, C_ROPE:C_ROPE + NT] = np.concatenate([-sin, sin])
    t = np.arange(P)
    cst[:, C_CAUSAL:C_CAUSAL + P] = np.where(t[None, :] <= t[:, None], 0.0, NEG)
    cst[:, C_INTRA:C_INTRA + P] = (t[:, None] <= t[None, :]) & (t[:, None] // CHUNK == t[None, :] // CHUNK)
    cst[:, C_CHUNK:C_CHUNK + CH_BLK] = t[:, None] // CHUNK == np.arange(CH_BLK)[None, :]
    cst[:, C_EPS] = EPS
    scan = np.broadcast_to((np.arange(SEQ) % CHUNK != 0).astype(np.float32), (P, SEQ))
    x = np.concatenate([i["x_prompt"].reshape(SEQ, D_MODEL), i["x_sample"].reshape(BATCH_D, D_MODEL)])
    lat = i["cache_ckv"][0]
    lat_t = lat.reshape(POOL, PAGE, CC, P).transpose(0, 3, 2, 1).reshape(POOL, P, CC * PAGE)
    cache = np.concatenate([lat_t, i["cache_kpe"][0], lat], axis=2)
    w_ukv = i["w_ukv"][0].reshape(KV_LORA, HEADS, NOPE + VDIM)
    return {
        "x": by_chunk(x).transpose(0, 2, 1), "w": w, "gain": gain, "cst": cst, "scan": scan, "cache": cache,
        "pages": i["page_table"].reshape(1, -1).astype(np.int32),
        "state": i["state_hgrn"][0].transpose(0, 2, 1, 3),
        "conv_st": by_chunk(i["state_conv"][0]).transpose(0, 3, 2, 1),
        "w_uk": w_ukv[:, :, :NOPE].transpose(2, 1, 0), "w_uv": w_ukv[:, :, NOPE:].reshape(CC, P, HEADS, VDIM).transpose(1, 0, 2, 3),
    }


OUTS = {"y": (P, KC, NT), "ckv": (P, CC, NT), "k_pe": (ROPE, NT), "state_p": (P, BH, P), "state_s": (BATCH_D, P, BH, P),
        "conv_p": (P, KC, 2), "conv_s": (P, KC, 2, BATCH_D)}


def kernel(**inputs):
    import concourse.bacc as bacc
    from concourse.bass_utils import run_bass_kernel_spmd

    i = {k: np.asarray(v) for k, v in inputs.items()}
    arrays = {f"in_{k}": np.ascontiguousarray(v) for k, v in lay_out(i).items()}
    nc = bacc.Bacc("TRN2", target_bir_lowering=False, num_devices=1)
    dram = {k[3:]: nc.dram_tensor(k, a.shape, mybir.dt.from_np(a.dtype), kind="ExternalInput").ap() for k, a in arrays.items()}
    for k, shape in OUTS.items():
        dram[k] = nc.dram_tensor(f"out_{k}", shape, F32, kind="ExternalOutput").ap()
    build(nc, dram)
    got = run_bass_kernel_spmd(nc, [arrays], core_ids=[0]).results[0]
    y, ckv, k_pe, state_p, state_s, conv_p, conv_s = (got[f"out_{k}"] for k in OUTS)
    y = y.transpose(2, 1, 0).reshape(NT, D_MODEL)
    ckv = ckv.transpose(2, 1, 0).reshape(NT, KV_LORA)
    k_pe = k_pe.T
    return (y[None, :SEQ], y[SEQ:, None],
            ckv[None, None, :SEQ], k_pe[None, None, :SEQ], ckv[None, SEQ:, None], k_pe[None, SEQ:, None],
            state_p.transpose(1, 0, 2)[None, None], state_s.transpose(0, 2, 1, 3)[None],
            conv_p.transpose(2, 1, 0).reshape(1, 1, 2, D_MODEL),
            conv_s.transpose(3, 2, 1, 0).reshape(1, BATCH_D, 2, D_MODEL))
```

```python
from contextlib import ExitStack

import numpy as np

import concourse.bass as bass
from concourse import mybir
from concourse.alu_op_type import AluOpType as ALU

F32 = mybir.dt.float32
F32R = mybir.dt.float32r
I32 = mybir.dt.int32
ACT = mybir.ActivationFunctionType
AX = mybir.AxisListType

P = 128
D_MODEL, SEQ, BATCH_D, D_FF = 1024, 512, 8, 2816
NP_TOK = SEQ
NT = SEQ + BATCH_D
HALF = NT // 2
KC = D_MODEL // P
FC = D_FF // P
HEADS, NOPE, ROPE, VDIM, Q_LORA, KV_LORA = 8, 64, 32, 64, 384, 256
QC, CC = Q_LORA // P, KV_LORA // P
BH, DK = 4, 128
CHUNK = 16
PAGE, PAGES, POOL = 128, 32, 320
SM_SCALE = (NOPE + ROPE) ** -0.5
EPS = 1e-6
NEG = -1e30

UNIT = 8 * P
DOWN_U = 3
GATE_UNITS = 2 * FC
FFN_UNITS = GATE_UNITS + KC * DOWN_U
FFN_GROUPS = GATE_UNITS + KC
AB_UNITS = 22
Z_Q, Z_G, Z_F, Z_I, Z_CQ, Z_CKV, Z_KPE = 0, 4, 8, 12, 16, 19, 21
UQ_UNITS, UKV_UNITS = 3, 2
C_UNITS = 3 * KC

PHASES = [("ffn0", FFN_UNITS, FFN_GROUPS), ("ab", AB_UNITS, AB_UNITS), ("uq", UQ_UNITS, HEADS),
          ("ukv", UKV_UNITS, 0), ("ab_out", KC, KC), ("ffn1", FFN_UNITS, FFN_GROUPS),
          ("ffn2", FFN_UNITS, FFN_GROUPS), ("c", C_UNITS, C_UNITS), ("c_out", KC, KC),
          ("ffn3", FFN_UNITS, FFN_GROUPS)]
U0, G0 = {}, {}
_u = _g = 0
for _name, _units, _groups in PHASES:
    U0[_name], G0[_name] = _u, _g
    _u, _g = _u + _units, _g + _groups
N_UNITS = _u
BLOCKS = SEQ // P
CH_BLK = P // CHUNK
GRP = 4
N_GRP = PAGES // GRP
G_ROWS = N_GRP * HEADS
JOB = 2
S_W = 2 * P + ROPE
RING, SPLITS = 6, 3
JOBS_SEQ = PAGES // JOB
S_JOBS = BATCH_D * JOBS_SEQ
LAG = JOBS_SEQ + 7
WINDOW = 3 * (G_ROWS - HEADS) + 2 * HEADS
assert N_UNITS % 3 == 0
READS = {"ffn0": 0, "ab": 1, "ffn1": 2, "ffn2": 3, "c": 4, "ffn3": 5}
FFN_NO = {"ffn0": 0, "ffn1": 1, "ffn2": 2, "ffn3": 3}

C_IDENT, C_ONES, C_ROPE, C_CAUSAL, C_INTRA, C_CHUNK, C_EPS, C_SEL, C_W = 0, 128, 256, 776, 904, 1032, 1040, 1041, 1057
G_NORM, G_FINAL, G_Q, G_KV, G_LB, G_OUT, G_CONV, G_W = 0, 48, 56, 59, 61, 73, 74, 98


def build(nc, dram):
    ctx = ExitStack()
    with ctx:
        sems = {}

        def S(name):
            if name not in sems:
                sems[name] = ctx.enter_context(nc.semaphore(name))
            return sems[name]

        top = [(nc.sbuf_base + 31) // 32 * 32]

        def tile(name, shape, dt=F32, offset=None):
            size = int(np.prod(shape[1:])) * 4
            if offset is None:
                offset = top[0]
                top[0] += (size + 31) // 32 * 32
            return nc.alloc_sbuf_tensor_at(f"sb_{name}", shape, dt, offset=offset)

        TOK = NT * 4
        x = tile("x", [P, KC, NT])
        raw = [tile(f"raw{i}", [P, 8, P]) for i in range(3)]
        w_hi = [tile(f"w_hi{i}", [P, 8, P], F32R) for i in range(3)]
        w_lo = [tile(f"w_lo{i}", [P, 8, P], F32R) for i in range(3)]
        at_t = top[0]
        t1, t2, t3, acc = [tile(n, [P, NT]) for n in ("t1", "t2", "t3", "acc")]
        r = tile("r", [P, NT])
        cst = tile("cst", [P, C_W])
        gain = tile("gain", [P, G_W])
        pages = tile("pages", [1, BATCH_D * PAGES], I32)
        conv_st = tile("conv_st", [P, KC, 2, BATCH_D])
        k_pe = tile("k_pe", [P, NT])
        rope_r = tile("rope_r", [P, NT])
        lb = tile("lb", [P, 4, BH])
        at_h = top[0]
        h_hi = tile("h_hi", [P, KC, NT], F32R)
        h_lo = tile("h_lo", [P, KC, NT], F32R)
        at_a = top[0]
        a_hi = tile("a_hi", [P, FC, NT], F32R)
        a_lo = tile("a_lo", [P, FC, NT], F32R)
        at_e = top[0]

        def tiles_at(start, *specs):
            out = []
            for name, shape, *dt in specs:
                out.append(tile(name, shape, dt[0] if dt else F32, offset=start))
                start += (int(np.prod(shape[1:])) * 4 + 31) // 32 * 32
            assert start <= nc.sbuf_usable_end, (name, start, nc.sbuf_usable_end)
            return out

        m_hi, m_lo = tiles_at(at_a + 28 * TOK, ("m_hi", [P, KC, NT], F32R), ("m_lo", [P, KC, NT], F32R))
        z, = tiles_at(at_a, ("z", [P, AB_UNITS, NT]))
        k_all, bcum, qe, ke, kd = tiles_at(at_a + 22 * TOK, ("k_all", [P, BH, NT]), ("bcum", [P, BH, SEQ]),
                                           ("qe", [P, BH, SEQ]), ("ke", [P, BH, SEQ]), ("kd", [P, BH, SEQ]))
        v_blk = tiles_at(at_a + 26 * TOK, ("v_blk0", [P, CH_BLK, P]), ("v_blk1", [P, CH_BLK, P]))
        o_fac, = tiles_at(at_a + 26 * TOK, ("o_fac", [P, BH, NT]))
        q_t, k_t, v_t, prob, prob_t = tiles_at(at_a, ("q_t", [P, HEADS, NT]), ("k_t", [P, HEADS, SEQ]),
                                               ("v_t", [P, BLOCKS, HEADS * VDIM]), ("prob", [P, 10, P]), ("prob_t", [P, 10, P]))
        cq_hi, cq_lo, ckv_hi, ckv_lo, squares = tiles_at(
            at_h, ("cq_hi", [P, QC, NT], F32R), ("cq_lo", [P, QC, NT], F32R), ("ckv_hi", [P, CC, NT], F32R),
            ("ckv_lo", [P, CC, NT], F32R), ("squares", [P, 4, NT]))
        st0, st1, v_diag, s_tmp = tiles_at(at_h + 10 * TOK, ("st0", [P, BH, P]), ("st1", [P, BH, P]),
                                           ("v_diag", [P, BH, P]), ("s_tmp", [P, BH, P]))
        st = [st0, st1]
        ckv, = tiles_at(at_h + 14 * TOK, ("ckv", [P, CC, NT]))
        rings = tiles_at(at_h, *[(f"s_raw{i}", [P, JOB, S_W]) for i in range(RING)],
                         *[(f"v_raw{i}", [P, JOB, KV_LORA]) for i in range(RING)],
                         ("self_row", [P, CC * P]), ("o_sb", [P, CC * P]), ("mx_p", [P, 2, BLOCKS]), ("sum_p", [P, 2, BLOCKS]),
                         ("mx", [P, 1]), ("mx_row", [P, HEADS]), ("mx_rep", [P, G_ROWS]), ("shift", [P, 1]),
                         ("row_sum", [P, 1]), ("inv0", [P, 1]), ("inv1", [P, 1]), ("own", [P, BATCH_D]),
                         ("p_own0", [P, 2 * HEADS]), ("p_own1", [P, 2 * HEADS]))
        s_raw, v_raw = rings[:RING], rings[RING:2 * RING]
        self_row, o_sb, mx_p, sum_p, mx, mx_row, mx_rep, shift, row_sum, inv0, inv1, own, p_own0, p_own1 = rings[2 * RING:]
        assert (2 * RING * JOB * P * 2 + RING * JOB * ROPE) * 4 < 14 * TOK
        inv, p_own = [inv0, inv1], [p_own0, p_own1]
        w_uv, = tiles_at(at_h, ("w_uv", [P, CC, HEADS, VDIM]))
        s_ring, kdv0, kdv1, att0, att1, decay = tiles_at(
            at_e, ("s_ring", [P, 2 * CH_BLK, P]), ("kdv0", [P, 2, P]), ("kdv1", [P, 2, P]), ("att0", [P, P]),
            ("att1", [P, P]), ("decay", [P, BH, SEQ // CHUNK]))
        kdv, att = [kdv0, kdv1], [att0, att1]
        c_parts = tiles_at(at_e, *[(f"c_{part}{i}", [P, JOB, S_W], F32R) for i in range(2) for part in ("hi", "lo")],
                           ("q_win", [P, CC + GRP, WINDOW], F32R))
        q_win = c_parts.pop()
        more = tiles_at(at_a + (HEADS * (NT + SEQ + BLOCKS * VDIM) + 20 * P) * 4, ("c_hi2", [P, JOB, S_W], F32R), ("c_lo2", [P, JOB, S_W], F32R),
                        ("q_s", [P, BATCH_D, CC + GRP, HEADS]), ("o_lat", [P, CC, HEADS, BATCH_D]))
        q_s, o_lat = more[2:]
        assert at_a + 28 * TOK >= at_a + (HEADS * (NT + SEQ + BLOCKS * VDIM) + 20 * P + 2 * JOB * S_W + 64 * HEADS) * 4
        c_hi, c_lo = c_parts[0::2] + [more[0]], c_parts[1::2] + [more[1]]
        s_all, s_lo, p_all, p_t0, p_t1 = tiles_at(
            at_t, ("s_all", [P, GRP * P + 1]), ("s_lo", [P, GRP * P]), ("p_all", [P, GRP * P + 1]),
            ("p_t0", [P, GRP, N_GRP, 2 * HEADS], F32R), ("p_t1", [P, GRP, N_GRP, 2 * HEADS], F32R))
        p_t = [p_t0, p_t1]
        s_fin, = tiles_at(at_t, ("s_fin", [P, BH, P]))
        w_uk, = tiles_at(at_t, ("w_uk", [NOPE, HEADS, KV_LORA]))
        v_ext, c_tail, c_last = tiles_at(at_a, ("v_ext", [P, 2 + NT]), ("c_tail", [P, KC, 2]), ("c_last", [P, KC, BATCH_D]))

        bank = [ctx.enter_context(nc.psum_tensor(f"bank{i}", [P, 512], F32)) for i in range(8)]
        ident = cst[:, C_IDENT:C_IDENT + P]
        ones = cst[:, C_ONES:C_ONES + P]
        sel = cst[:, C_SEL:C_SEL + 2 * HEADS]
        p_turned = bank[3][:, 0:GRP * G_ROWS].rearrange("p (j g h) -> p j g h", j=GRP, h=HEADS)

        half = [slice(0, HALF), slice(HALF, NT)]

        def pair(g, hf):
            return bank[2 * (g % 3) + hf][:, 0:HALF]

        def split_hi(n0, step=None):
            n = n0 if step is None else n0 + step
            slot = n0 % 3
            nc.scalar.wait_ge(S(f"w_loaded{slot}"), 16 * (n0 // 3 + 1) if step is None else 16 * (n0 // 3 + 1) + step_loads(step))
            if step is not None or n0 >= 3:
                nc.scalar.wait_ge(S("half_done"), 2 * n - 4)
            nc.scalar.activation(w_hi[slot][:], raw[slot][:], ACT.Copy).then_inc(S("w_hi_done"), 1)

        def split_lo(n0, step=None):
            n = n0 if step is None else n0 + step
            slot = n0 % 3
            nc.vector.wait_ge(S("w_hi_done"), n + 1)
            nc.vector.tensor_tensor(w_lo[slot][:], raw[slot][:], w_hi[slot][:], ALU.subtract).then_inc(S("w_lo_done"), 1)

        def step_loads(step):
            return step.loads

        class Step:

            def __init__(self, i, k):
                assert k % 3 == 0
                self.i, self.k = i, k
                self.loads = i * (16 * k // 3)

            def __radd__(self, n):
                return n + self.i * self.k

        def multiply(slot, g, hi, lo, k0, chunks, first, last, wait_chunk=None):
            for hf in range(2):
                out = pair(g, hf)
                for c in range(chunks):
                    if wait_chunk:
                        wait_chunk(c, hf)
                    xh, xl = hi[:, k0 + c, half[hf]], lo[:, k0 + c, half[hf]]
                    wh, wl = w_hi[slot][:, c, :], w_lo[slot][:, c, :]
                    nc.tensor.matmul(out, wh, xh, start=first and c == 0, stop=False)
                    nc.tensor.matmul(out, wh, xl, start=False, stop=False)
                    mm = nc.tensor.matmul(out, wl, xh, start=False, stop=last and c == chunks - 1)
                mm.then_inc(S("half_done"), 1)

        def unit_ready(n):
            nc.tensor.wait_ge(S("w_lo_done"), n + 1)

        def group_free(g):
            nc.tensor.wait_ge(S("drained"), 2 * g - 4)

        def norm_sum(res):
            for hf in range(2):
                nc.tensor.wait_ge(S("squares_added"), 14 * res + 13 + hf)
                nc.tensor.matmul(bank[6 + hf][:, 0:HALF], ones, acc[:, half[hf]], start=True, stop=True) \
                    .then_inc(S("norm_summed"), 1)

        def inverse_root(out, sums, n, width):
            nc.scalar.activation(out, sums, ACT.Ln, bias=cst[:, C_EPS:C_EPS + 1], scale=1.0 / width) \
                .then_inc(S("log_taken"), 1)
            nc.scalar.wait_ge(S("log_taken"), n + 1)
            nc.scalar.activation(out, out, ACT.Exp, scale=-0.5).then_inc(S("factor"), 1)

        def norm_factor(res):
            for hf in range(2):
                nc.scalar.wait_ge(S("norm_summed"), 2 * res + hf + 1)
                inverse_root(r[:, half[hf]], bank[6 + hf][:, 0:HALF], factors_before(res) + hf, D_MODEL)

        def factors_before(res):
            return 2 * res + (4 if res > 1 else 0)

        def factor_ready(res):
            nc.vector.wait_ge(S("factor"), factors_before(res) + 2)

        def chunk_act(res, d, dd, split=True):
            for hf in range(2):
                n = res * 16 + 2 * dd + hf + 1
                if res:
                    nc.scalar.wait_ge(S("x_added"), n - 16)
                src = x[:, dd, half[hf]]
                if split:
                    nc.scalar.activation(h_hi[:, dd, half[hf]], src, ACT.Copy,
                                         scale=gain[:, bass.ds(G_NORM + 8 * res + dd, 1)]).then_inc(S("h_hi_done"), 1)
                to = acc if isinstance(d, int) and d == 0 else t2
                if not res and d >= 2:
                    nc.scalar.wait_ge(S("squares_added"), 2 * (d - 2) + hf + 1)
                nc.scalar.activation(to[:, half[hf]], src, ACT.Square).then_inc(S("squared"), 1)

        def chunk_dve(res, d, dd, split=True):
            for hf in range(2):
                n = res * 16 + 2 * dd + hf + 1
                if split:
                    nc.vector.wait_ge(S("h_hi_done"), n)
                    nc.vector.scalar_tensor_tensor(h_lo[:, dd, half[hf]], x[:, dd, half[hf]],
                                                   gain[:, bass.ds(G_NORM + 8 * res + dd, 1)],
                                                   h_hi[:, dd, half[hf]], op0=ALU.mult, op1=ALU.subtract) \
                        .then_inc(S("h_lo_done"), 1)
                nc.vector.wait_ge(S("squared"), n)
                if not (isinstance(d, int) and d == 0):
                    nc.vector.tensor_tensor(acc[:, half[hf]], acc[:, half[hf]], t2[:, half[hf]], ALU.add) \
                        .then_inc(S("squares_added"), 1)

        def add_residual(res, dd, g, n_last, scaled):
            for hf in range(2):
                xs = x[:, dd, half[hf]]
                nc.vector.wait_ge(S("half_done"), 2 * n_last + hf + 1)
                if scaled:
                    nc.vector.scalar_tensor_tensor(t1[:, half[hf]], pair_at(g, hf), 0.5, r[:, half[hf]],
                                                   op0=ALU.mult, op1=ALU.mult).then_inc(S("drained"), 1)
                else:
                    nc.vector.tensor_copy(t1[:, half[hf]], pair_at(g, hf)).then_inc(S("drained"), 1)
            for hf in range(2):
                xs = x[:, dd, half[hf]]
                nc.vector.wait_ge(S("drained"), 2 * g[1] + hf + 1)
                nc.vector.tensor_tensor(xs, xs, t1[:, half[hf]], ALU.add).then_inc(S("x_added"), 1)

        def pair_at(g, hf):
            return pair(g[0], hf)

        def at(static, moving=0):
            return (static, static + moving)

        def over(eng, peel, total, per, body, tail=0):
            for d in range(peel):
                body(d, 1, 0)
            assert (total - peel - tail) % per == 0
            with eng.Fori(0, (total - peel - tail) // per) as i:
                body(peel, per, i)
            for d in range(total - tail, total):
                body(d, 1, 0)

        block = ctx.enter_context(nc.Block())
        GATE_PEEL, OUT_PEEL, C_PEEL, Z_PEEL = 1, 2, 1, 1
        LAST = "ffn3"
        IN_PHASES = ("ffn0", "ab", "ab_out", "ffn1", "ffn2", "c", "c_out", "ffn3")

        def tail(name):
            return 3 if name == LAST else 0

        def o_block(h, b):
            return slice(b * P, (b + 1) * P)

        def tri(b):
            return b * (b + 1) // 2

        score_at = [bank[5][:, 0:P], bank[5][:, P:3 * P], bank[6][:, 0:3 * P], bank[7][:, 0:4 * P]]

        def s_job(k):
            return k + max(0, k - LAG)

        def v_job(k):
            return k + min(S_JOBS, k + LAG + 1)

        def load_pages(eng, kind, slots, lo, width, number):
            for k in range(S_JOBS):
                if k >= RING:
                    eng.wait_ge(S("c_lo_done"), number(k - RING) + 1)
                for j in range(JOB):
                    at_page = k * JOB + j
                    page = eng.value_load(pages[0:1, at_page:at_page + 1], min_val=0, max_val=POOL - 1)
                    eng.dma_start(slots[k % RING][:, j, :],
                                  dram["cache"][bass.ds(page, 1), :, lo:lo + width].rearrange("a p w -> (a p) w")) \
                        .then_inc(S(f"{kind}_loaded{k % RING}"), 16)

        @block.sync
        def _(sp):
            def stream(n_first, n_end):
                with sp.Fori(0, (n_end - n_first) // 3) as i:
                    for k in range(3):
                        sp.wait_ge(S("w_lo_done"), 3 * i + (n_first + k - 2))
                        sp.dma_start(raw[k][:].rearrange("p c m -> p (c m)"), dram["w"][3 * i + (n_first + k)]) \
                            .then_inc(S(f"w_loaded{k}"), 16)

            sp.dma_start(x[:], dram["x"]).then_inc(S("x_loaded"), 16)
            sp.dma_start(gain[:], dram["gain"]).then_inc(S("gain_loaded"), 16)
            for n in range(3):
                sp.dma_start(raw[n][:].rearrange("p c m -> p (c m)"), dram["w"][n]).then_inc(S(f"w_loaded{n}"), 16)
            sp.dma_start(cst[:], dram["cst"]).then_inc(S("cst_loaded"), 16)
            sp.dma_start(pages[:], dram["pages"]).then_inc(S("pages_loaded"), 16)

            n_cache = -(-(U0["ab_out"] + 3) // 3) * 3
            stream(3, n_cache)
            sp.wait_ge(S("pages_loaded"), 16)
            sp.wait_ge(S("v_kept"), BLOCKS)
            sp.wait_ge(S("k_done"), HEADS)
            load_pages(sp, "s", s_raw, 0, S_W, s_job)
            stream(n_cache, N_UNITS)
            for n in range(KC):
                sp.wait_ge(S("y_ready"), n + 1)
                sp.dma_start(dram["y"][:, n], x[:, n, :]).then_inc(S("y_stored"), 16)
            sp.wait_ge(S("y_stored"), 16 * KC)

        @block.gpsimd
        def _(pool):
            for i in range(2):
                pool.memset(att[i][:], 0.0).then_inc(S("att_zeroed"), 1)
            pool.dma_start(conv_st[:], dram["conv_st"]).then_inc(S("conv_st_loaded"), 16)
            pool.wait_ge(S("conv_st_loaded"), 16)
            pool.dma_start(dram["conv_s"][:, :, 0, :], conv_st[:, :, 1, :]).then_inc(S("conv_old_stored"), 16)
            pool.wait_ge(S("drained"), 2 * (G0["ab"] + 1))
            pool.dma_start(t3[:, 0:SEQ], dram["scan"]).then_inc(S("scan_loaded"), 16)
            pool.wait_ge(S("ckv_ready"), CC)
            pool.dma_start(dram["ckv"], ckv[:]).then_inc(S("ckv_stored"), 16)
            pool.wait_ge(S("k_pe_step"), 3)
            pool.dma_start(dram["k_pe"], k_pe[NOPE:NOPE + ROPE, :]).then_inc(S("k_pe_stored"), 16)
            for b in range(BATCH_D):
                if b == 0:
                    pool.wait_ge(S("cq_summed"), 4)
                if b >= 2:
                    pool.wait_ge(S("os_mm"), b - 1)
                    pool.wait_ge(S(f"st_stored{b % 2}"), 16 * (b // 2))
                pool.dma_start(st[b % 2][:], dram["state"][b]).then_inc(S(f"st_loaded{b % 2}"), 16)
                if b >= 1:
                    pool.wait_ge(S("s_new"), b)
                    pool.dma_start(dram["state_s"][b - 1], st[(b - 1) % 2][:]).then_inc(S(f"st_stored{(b - 1) % 2}"), 16)
                if b == 0:
                    pool.wait_ge(S("final_kept"), BH)
                    pool.dma_start(dram["state_p"], s_fin[:]).then_inc(S("s_fin_stored"), 16)
            pool.wait_ge(S("s_new"), BATCH_D)
            pool.dma_start(dram["state_s"][BATCH_D - 1], st[1][:]).then_inc(S("st_stored1"), 16)
            pool.wait_ge(S("q_ready"), 2 * HEADS)
            pool.dma_start(w_uk[:], dram["w_uk"]).then_inc(S("w_uk_loaded"), 16)
            pool.memset(q_s[:], 0.0).then_inc(S("q_s_cleared"), 1)
            pool.memset(q_win[:].bitcast(F32), 0.0).then_inc(S("att_cleared"), 1)
            for b in range(2):
                pool.memset(p_own[b][:], 0.0).then_inc(S("att_cleared"), 1)
            pool.wait_ge(S("pages_loaded"), 16)
            pool.wait_ge(S("v_kept"), BLOCKS)
            pool.wait_ge(S("k_done"), HEADS)
            load_pages(pool, "v", v_raw, S_W, KV_LORA, v_job)
            pool.dma_start(w_uv[:], dram["w_uv"]).then_inc(S("w_uv_loaded"), 16)
            pool.wait_ge(S("conv_kept"), 2 * KC)
            pool.dma_start(dram["conv_p"], c_tail[:]).then_inc(S("conv_p_stored"), 16)
            pool.dma_start(dram["conv_s"][:, :, 1, :], c_last[:]).then_inc(S("conv_s_stored"), 16)
            for name in ("ckv", "k_pe", "s_fin", "conv_old", "conv_p", "conv_s"):
                pool.wait_ge(S(f"{name}_stored"), 16)
            for i in range(2):
                pool.wait_ge(S(f"st_stored{i}"), 16 * BATCH_D // 2)

        @block.scalar
        def _(act):
            def prefetch(n, step=None):
                if n + 3 < N_UNITS:
                    split_hi(n + 3, step)

            def ffn(name):
                n0, g0, res = U0[name], G0[name], READS[name]

                def gate_up(f0, count, i):
                    st = None if isinstance(i, int) else Step(i, 2 * count)
                    for f in range(f0, f0 + count):
                        ff = f if st is None else f + i * count
                        n, gg = n0 + 2 * f, g0 + 2 * ff
                        if st is None and f == 0:
                            norm_factor(res)
                        prefetch(n, st)
                        for hf in range(2):
                            act.wait_ge(S("drained"), 2 * gg + hf + 1)
                            act.activation(t2[:, half[hf]], t1[:, half[hf]], ACT.Silu).then_inc(S("silu_done"), 1)
                        prefetch(n + 1, st)
                        for hf in range(2):
                            act.wait_ge(S("drained"), 2 * gg + 2 + hf + 1)
                            act.activation(a_hi[:, ff, half[hf]], t3[:, half[hf]], ACT.Copy).then_inc(S("a_hi_done"), 1)

                over(act, GATE_PEEL, FC, 3, gate_up)
                n0 += GATE_UNITS

                def down(d0, count, i):
                    st = None if isinstance(i, int) else Step(i, 3 * count)
                    for d in range(d0, d0 + count):
                        for u in range(DOWN_U):
                            prefetch(n0 + 3 * d + u, st)
                        chunk_act(res + 1, d, d if st is None else d + i * count, split=name != LAST)

                over(act, OUT_PEEL, KC, 3, down, tail(name))

            def out_projection(name, res):
                n0 = U0[name]

                def column(d0, count, i):
                    st = None if isinstance(i, int) else Step(i, count)
                    for d in range(d0, d0 + count):
                        prefetch(n0 + d, st)
                        chunk_act(res, d, d if st is None else d + i * count)

                over(act, OUT_PEEL, KC, 3, column)

            def ab_in():
                n0, g0 = U0["ab"], G0["ab"]

                def column(u0, count, i):
                    st = None if isinstance(i, int) else Step(i, count)
                    for u in range(u0, u0 + count):
                        if st is None:
                            norm_factor(READS["ab"])
                        prefetch(n0 + u, st)

                over(act, Z_PEEL, Z_CQ, 3, column)
                prefetch(n0 + 16)
                for n, z0 in enumerate((Z_Q, Z_G)):
                    act.wait_ge(S("drained"), 2 * (g0 + z0 + BH))
                    act.activation(z[:, z0:z0 + BH, :], z[:, z0:z0 + BH, :], ACT.Silu).then_inc(S("silus"), 1)
                prefetch(n0 + 17)
                act.wait_ge(S("drained"), 2 * (g0 + Z_F + BH))
                act.activation(z[:, Z_F:Z_F + BH, :], z[:, Z_F:Z_F + BH, :], ACT.Sigmoid).then_inc(S("f_sigmoid"), 1)
                prefetch(n0 + 18)
                act.wait_ge(S("f_scaled"), BH)
                act.activation(qe[:], z[:, Z_F:Z_F + BH, 0:SEQ], ACT.Ln).then_inc(S("log_f"), 1)
                prefetch(n0 + 19)
                act.wait_ge(S("cum_done"), BH)
                act.activation(qe[:], bcum[:], ACT.Exp).then_inc(S("exp_cum"), 1)
                act.activation(ke[:], bcum[:], ACT.Exp, scale=-1.0).then_inc(S("exp_cum"), 1)
                prefetch(n0 + 20)
                act.wait_ge(S("to_end"), 1)
                act.activation(kd[:], kd[:], ACT.Exp).then_inc(S("exp_cum"), 1)
                prefetch(n0 + 21)
                for c in range(QC):
                    act.wait_ge(S("drained"), 2 * (g0 + Z_CQ + c + 1))
                    act.activation(cq_hi[:, c, :], z[:, Z_CQ + c, :], ACT.Copy, scale=gain[:, G_Q + c:G_Q + c + 1]) \
                        .then_inc(S("cq_hi_done"), 1)
                    act.activation(squares[:, c, :], z[:, Z_CQ + c, :], ACT.Square).then_inc(S("c_squared"), 1)
                for c in range(CC):
                    act.wait_ge(S("drained"), 2 * (g0 + Z_CKV + c + 1))
                    act.activation(squares[:, 3, :] if c == 0 else acc[:], z[:, Z_CKV + c, :], ACT.Square) \
                        .then_inc(S("c_squared"), 1)
                n = factors_before(1) + 2
                for k, (to, width) in enumerate(((r, Q_LORA), (t3, KV_LORA))):
                    act.wait_ge(S("drained"), 2 * (g0 + AB_UNITS))
                    for hf in range(2):
                        act.wait_ge(S("cq_summed"), 2 * k + hf + 1)
                        inverse_root(to[:, half[hf]], bank[6 + hf][:, 0:HALF], n + 2 * k + hf, width)

            def hgrn():
                def keep(m):
                    act.wait_ge(S("kv_transposed"), m + 1)
                    if m >= 2:
                        act.wait_ge(S("o_mm"), m - 1)
                    act.activation(kdv[m % 2][:].rearrange("p a d -> p (a d)"), bank[m % 2][:, 0:2 * P], ACT.Copy).then_inc(S("kv_kept"), 1)

                keep(0)
                for m in range(BH * BLOCKS):
                    h, b = divmod(m, BLOCKS)
                    if m + 1 < BH * BLOCKS:
                        keep(m + 1)
                    act.wait_ge(S("o_mm"), m + 1)
                    act.activation(z[:, Z_Q + h, o_block(h, b)], bank[6 + m % 2][:, 0:P], ACT.Copy).then_inc(S("o_kept"), 1)
                    if m == 0:
                        act.wait_ge(S("ckv_ready"), CC)
                        act.activation(ckv_hi[:], ckv[:], ACT.Copy).then_inc(S("ckv_hi_done"), 1)
                act.wait_ge(S("os_kept"), 1)
                act.activation(k_all[:], z[:, Z_Q:Z_Q + BH, :], ACT.Square).then_inc(S("o_squared"), 1)
                for h in range(BH):
                    for hf in range(2):
                        act.wait_ge(S("o_summed"), 2 * h + hf + 1)
                        act.activation(o_fac[:, h, half[hf]], bank[2 * h + hf][:, 0:HALF], ACT.Ln,
                                       bias=cst[:, C_EPS:C_EPS + 1], scale=1.0 / DK).then_inc(S("o_log"), 1)
                act.wait_ge(S("o_log"), 2 * BH)
                act.activation(o_fac[:], o_fac[:], ACT.Exp, scale=-0.5).then_inc(S("o_factor"), 1)
                act.wait_ge(S("o_step"), 2)
                act.activation(m_hi[:, BH:, :], z[:, Z_Q:Z_Q + BH, :], ACT.Copy).then_inc(S("mix_hi_done"), 1)

            def qkv():
                n0 = U0["uq"]
                for h in range(HEADS):
                    if h in (2, 5, 7):
                        prefetch(n0 + (2, 5, 7).index(h))
                act.wait_ge(S("k_pe_step"), 3)
                act.wait_ge(S("q_ready"), 1)
                for h in range(HEADS):
                    act.activation(k_t[NOPE:NOPE + ROPE, h, :], k_pe[NOPE:NOPE + ROPE, 0:SEQ], ACT.Copy).then_inc(S("k_kept"), 1)
                for h in range(HEADS):
                    act.wait_ge(S("k_done"), h + 1)
                    act.activation(k_t[0:NOPE, h, :], bank[h % 4][0:NOPE, :], ACT.Copy).then_inc(S("k_kept"), 1)
                for u in range(UKV_UNITS):
                    prefetch(U0["ukv"] + u)

            def attention():
                def split(kind, slots, width, k, n):
                    act.wait_ge(S(f"{kind}_loaded{k % RING}"), 16 * JOB * (k // RING + 1))
                    if n >= SPLITS:
                        act.wait_ge(S("job_done"), n - SPLITS + 1)
                    act.activation(c_hi[n % SPLITS][:, :, 0:width], slots[k % RING][:], ACT.Copy).then_inc(S("c_hi_done"), 1)

                def queries(i):
                    if i == 0:
                        act.wait_ge(S("att_cleared"), 3)
                        act.wait_ge(S("q_s_ready"), 1 + GRP)
                    else:
                        act.wait_ge(S("job_done"), s_job(JOBS_SEQ * i - 1) + 1)
                    act.activation(q_win[:, :, G_ROWS - HEADS:G_ROWS], q_s[:, i], ACT.Copy).then_inc(S("q_win_hi"), 1)

                def prompt(i, t):
                    if 5 <= t < 9:
                        b = t - 5
                        act.wait_ge(S("max_scaled"), i + 1)
                        if b == 0 and i:
                            act.wait_ge(S("p_transposed"), 3 * i)
                        act.activation(prob[:, tri(b):tri(b + 1), :].rearrange("p a k -> p (a k)"), score_at[b], ACT.Exp,
                                       bias=mx_p[:, 1, b:b + 1], scale=SM_SCALE, accum_out=sum_p[:, 0, b:b + 1]) \
                            .then_inc(S("p_exp"), 1)
                    if 11 <= t < 14:
                        e = t - 11
                        act.wait_ge(S("p_transposed"), 3 * i + e + 1)
                        if e == 0 and i:
                            act.wait_ge(S("o_a_mm"), i)
                        size = (4, 4, 2)[e]
                        act.activation(prob_t[:, 4 * e:4 * e + size, :].rearrange("p a k -> p (a k)"),
                                       bank[5 + e][:, 0:size * P], ACT.Copy).then_inc(S("pt_kept"), 1)
                    if t == 15:
                        rows = slice(i % 2 * VDIM, (i % 2 + 1) * VDIM)
                        act.wait_ge(S("o_a_mm"), i + 1)
                        act.activation(m_hi[rows, i // 2, 0:SEQ], bank[4][rows, :], ACT.Copy).then_inc(S("oa_hi_done"), 1)

                def softmax(i, d):
                    if d == 1:
                        act.wait_ge(S("job_done"), s_job(JOBS_SEQ * (i + 1) - 1) + 1)
                        if i:
                            act.wait_ge(S("s_added"), i)
                        act.activation(s_lo[0:G_ROWS, :], bank[i % 2][G_ROWS:P, :], ACT.Copy).then_inc(S("s_lo_kept"), 1)
                    if d == 5:
                        act.wait_ge(S("shift_ready"), i + 1)
                        if i:
                            act.wait_ge(S("p_turned"), i)
                        act.activation(p_all[0:G_ROWS, :], s_all[0:G_ROWS, :], ACT.Exp, bias=shift[0:G_ROWS, :], scale=SM_SCALE,
                                       accum_out=row_sum[0:G_ROWS, :]).then_inc(S("s_exp"), 1)
                    if d == 6:
                        act.wait_ge(S("p_turned"), i + 1)
                        if i >= 2:
                            act.wait_ge(S("pv_done"), i - 1)
                        act.activation(p_t[i % 2][:, :, :, 0:HEADS], p_turned, ACT.Copy).then_inc(S("p_hi_kept"), 1)
                        act.activation(p_own[i % 2][0:1, 0:HEADS], bank[3][0:1, 256:256 + HEADS], ACT.Copy).then_inc(S("p_hi_kept"), 1)
                    if d == 10:
                        act.wait_ge(S("self_turned"), i + 1)
                        if i:
                            act.wait_ge(S("pv_done"), i)
                        act.activation(self_row[0:1, :], bank[3][0:1, 0:CC * P], ACT.Copy).then_inc(S("self_kept"), 1)

                queries(0)
                for k in range(S_JOBS + LAG):
                    if k < S_JOBS:
                        split("s", s_raw, S_W, k, s_job(k))
                        prompt(*divmod(k, JOBS_SEQ))
                    if k >= LAG:
                        split("v", v_raw, KV_LORA, k - LAG, v_job(k - LAG))
                    if JOBS_SEQ <= k < S_JOBS + JOBS_SEQ:
                        softmax(k // JOBS_SEQ - 1, k % JOBS_SEQ + 1)
                    if k % JOBS_SEQ == 0 and 0 < k < S_JOBS:
                        queries(k // JOBS_SEQ)
                for i in range(HEADS):
                    rows = slice(i % 2 * VDIM, (i % 2 + 1) * VDIM)
                    act.wait_ge(S("os_a_mm"), 1)
                    act.activation(m_hi[rows, i // 2, SEQ:NT], bank[0][rows, i * BATCH_D:(i + 1) * BATCH_D], ACT.Copy) \
                        .then_inc(S("oa_hi_done"), 1)

            def conv():
                n0, g0 = U0["c"], G0["c"]

                def chunk(j0, count, i):
                    st = None if isinstance(i, int) else Step(i, 3)
                    j = j0
                    jj = j if st is None else j + i
                    if st is None:
                        norm_factor(READS["c"])
                    for u in range(3):
                        prefetch(n0 + 3 * j + u, st)
                        if u == 1:
                            act.wait_ge(S("v_ready"), 2 * jj + 2)
                            act.activation(c_tail[:, jj, :], v_ext[:, SEQ:SEQ + 2], ACT.Copy).then_inc(S("conv_kept"), 1)
                            act.activation(c_last[:, jj, :], v_ext[:, 2 + SEQ:2 + NT], ACT.Copy).then_inc(S("conv_kept"), 1)
                    act.wait_ge(S("c_gated"), jj + 1)
                    act.activation(m_hi[:, jj, :], t1[:], ACT.Copy).then_inc(S("mix_hi_done"), 1)

                over(act, C_PEEL, KC, 1, chunk)

            act.wait_ge(S("x_loaded"), 16)
            act.wait_ge(S("gain_loaded"), 16)
            for d in range(KC):
                chunk_act(0, d, d)
            for n in range(3):
                split_hi(n)
            act.wait_ge(S("lb_step"), 3)
            act.activation(lb[:, 0:3, :], lb[:, 0:3, :], ACT.Exp).then_inc(S("lb_exp"), 1)
            act.wait_ge(S("cst_loaded"), 16)
            ffn("ffn0")
            ab_in()
            hgrn()
            qkv()
            attention()
            out_projection("ab_out", 2)
            ffn("ffn1")
            ffn("ffn2")
            conv()
            out_projection("c_out", 5)
            act.wait_ge(S("conv_p_stored"), 16)
            act.wait_ge(S("conv_s_stored"), 16)
            ffn("ffn3")
            norm_factor(6)

        @block.vector
        def _(dve):
            def prefetch(n, step=None):
                if n + 3 < N_UNITS:
                    split_lo(n + 3, step)

            def ffn(name):
                n0, g0, res, no = U0[name], G0[name], READS[name], FFN_NO[name]

                def gate_up(f0, count, i):
                    st = None if isinstance(i, int) else Step(i, 2 * count)
                    for f in range(f0, f0 + count):
                        ff = f if st is None else f + i * count
                        n, g = n0 + 2 * f, g0 + 2 * f
                        nn = n0 + 2 * ff
                        if st is None and f == 0:
                            factor_ready(res)
                        for hf in range(2):
                            dve.wait_ge(S("half_done"), 2 * nn + hf + 1)
                            dve.tensor_tensor(t1[:, half[hf]], pair(g, hf), r[:, half[hf]], ALU.mult) \
                                .then_inc(S("drained"), 1)
                        prefetch(n, st)
                        for hf in range(2):
                            dve.wait_ge(S("half_done"), 2 * nn + 2 + hf + 1)
                            dve.wait_ge(S("silu_done"), (no * FC + ff) * 2 + hf + 1)
                            dve.tensor_tensor(t3[:, half[hf]], pair(g + 1, hf), t2[:, half[hf]], ALU.mult) \
                                .then_inc(S("drained"), 1)
                        prefetch(n + 1, st)
                        for hf in range(2):
                            dve.wait_ge(S("a_hi_done"), (no * FC + ff) * 2 + hf + 1)
                            dve.tensor_tensor(a_lo[:, ff, half[hf]], t3[:, half[hf]], a_hi[:, ff, half[hf]], ALU.subtract) \
                                .then_inc(S("a_lo_done"), 1)

                over(dve, GATE_PEEL, FC, 3, gate_up)
                n0 += GATE_UNITS
                g0 += GATE_UNITS

                def down(d0, count, i):
                    st = None if isinstance(i, int) else Step(i, 3 * count)
                    for d in range(d0, d0 + count):
                        dd = d if st is None else d + i * count
                        for u in range(DOWN_U - 1):
                            prefetch(n0 + 3 * d + u, st)
                        add_residual(res + 1, dd, (g0 + d, g0 + dd), n0 + 3 * dd + 2, scaled=True)
                        prefetch(n0 + 3 * d + 2, st)
                        chunk_dve(res + 1, d, dd, split=name != LAST)

                over(dve, OUT_PEEL, KC, 3, down, tail(name))

            def out_projection(name, res):
                n0, g0 = U0[name], G0[name]

                def column(d0, count, i):
                    st = None if isinstance(i, int) else Step(i, count)
                    for d in range(d0, d0 + count):
                        dd = d if st is None else d + i * count
                        add_residual(res, dd, (g0 + d, g0 + dd), n0 + dd, scaled=False)
                        prefetch(n0 + d, st)
                        chunk_dve(res, d, dd)

                over(dve, OUT_PEEL, KC, 3, column)

            def ab_in():
                n0, g0 = U0["ab"], G0["ab"]

                def drain(u, uu):
                    for hf in range(2):
                        dve.wait_ge(S("half_done"), 2 * (n0 + uu) + hf + 1)
                        dve.tensor_tensor(z[:, uu, half[hf]], pair(g0 + u, hf), r[:, half[hf]], ALU.mult) \
                            .then_inc(S("drained"), 1)

                def column(u0, count, i):
                    st = None if isinstance(i, int) else Step(i, count)
                    for u in range(u0, u0 + count):
                        if st is None:
                            factor_ready(READS["ab"])
                        drain(u, u if st is None else u + i * count)
                        prefetch(n0 + u, st)

                over(dve, Z_PEEL, Z_CQ, 3, column)
                drain(16, 16)
                prefetch(n0 + 16)
                drain(17, 17)
                prefetch(n0 + 17)
                f_all = z[:, Z_F:Z_F + BH, :]
                dve.wait_ge(S("f_sigmoid"), 1)
                for h in range(BH):
                    dve.tensor_scalar(z[:, Z_F + h, :], z[:, Z_F + h, :], lb[:, 3, h:h + 1], lb[:, 2, h:h + 1], ALU.mult, ALU.add) \
                        .then_inc(S("f_scaled"), 1)
                dve.wait_ge(S("f_scaled"), BH)
                dve.tensor_scalar(k_all[:], f_all, -1.0, 1.0, ALU.mult, ALU.add).then_inc(S("k_all_ready"), 1)
                drain(18, 18)
                prefetch(n0 + 18)
                dve.wait_ge(S("log_f"), 1)
                dve.wait_ge(S("scan_loaded"), 16)
                for h in range(BH):
                    dve.tensor_tensor_scan(bcum[:, h, :], t3[:, 0:SEQ], qe[:, h, :], 0.0, ALU.mult, ALU.add).then_inc(S("cum_done"), 1)
                drain(19, 19)
                prefetch(n0 + 19)
                by_chunk = "p h (n t) -> p (h n) t"
                b4 = bcum[:].rearrange(by_chunk, t=CHUNK)
                dve.wait_ge(S("cum_done"), BH)
                dve.tensor_tensor(kd[:].rearrange(by_chunk, t=CHUNK),
                                  b4[:, :, CHUNK - 1:CHUNK].to_broadcast([P, BH * SEQ // CHUNK, CHUNK]), b4, ALU.subtract) \
                    .then_inc(S("to_end"), 1)
                drain(20, 20)
                prefetch(n0 + 20)
                dve.wait_ge(S("exp_cum"), 1)
                dve.tensor_copy(decay[:].rearrange("p h n -> p (h n)"), qe[:].rearrange(by_chunk, t=CHUNK)[:, :, CHUNK - 1]) \
                    .then_inc(S("gates_ready"), 1)
                dve.wait_ge(S("silus"), 1)
                dve.tensor_scalar(z[:, Z_Q:Z_Q + BH, SEQ:NT], z[:, Z_Q:Z_Q + BH, SEQ:NT], DK ** -0.5, None, ALU.mult) \
                    .then_inc(S("gates_ready"), 1)
                dve.wait_ge(S("gates_ready"), 2)
                dve.scalar_tensor_tensor(qe[:], z[:, Z_Q:Z_Q + BH, 0:SEQ], DK ** -0.5, qe[:], op0=ALU.mult, op1=ALU.mult) \
                    .then_inc(S("gates_ready"), 1)
                drain(21, 21)
                prefetch(n0 + 21)
                for n, t in enumerate((ke, kd)):
                    dve.wait_ge(S("exp_cum"), n + 2)
                    dve.wait_ge(S("k_all_ready"), 1)
                    dve.tensor_tensor(t[:], k_all[:, :, 0:SEQ], t[:], ALU.mult).then_inc(S("gates_ready"), 1)
                for c in range(QC):
                    dve.wait_ge(S("cq_hi_done"), c + 1)
                    dve.scalar_tensor_tensor(cq_lo[:, c, :], z[:, Z_CQ + c, :], gain[:, G_Q + c:G_Q + c + 1], cq_hi[:, c, :],
                                             op0=ALU.mult, op1=ALU.subtract).then_inc(S("cq_lo_done"), 1)
                pe_rows, sw_rows = slice(NOPE, NOPE + ROPE), slice(NOPE + ROPE, P)
                dve.wait_ge(S("drained"), 2 * (g0 + AB_UNITS))
                dve.tensor_tensor(t1[pe_rows, :], z[pe_rows, Z_KPE, :], cst[pe_rows, C_ROPE:C_ROPE + NT], ALU.mult).then_inc(S("k_pe_step"), 1)
                dve.tensor_tensor(t2[pe_rows, :], z[sw_rows, Z_KPE, :], cst[sw_rows, C_ROPE:C_ROPE + NT], ALU.mult).then_inc(S("k_pe_step"), 1)
                dve.wait_ge(S("k_pe_step"), 2)
                dve.tensor_tensor(k_pe[pe_rows, :], t1[pe_rows, :], t2[pe_rows, :], ALU.add).then_inc(S("k_pe_step"), 1)

            def hgrn():
                chunk_mask = cst[:, C_CHUNK:C_CHUNK + CH_BLK]
                intra = cst[:, C_INTRA:C_INTRA + P].bitcast(I32)

                def masked(m):
                    dve.wait_ge(S("kv_kept"), m + 1)
                    if m >= 2:
                        dve.wait_ge(S("o_mm"), m - 1)
                    dve.tensor_tensor(v_blk[m % 2][:], kdv[m % 2][:, 1:2, :].to_broadcast([P, CH_BLK, P]),
                                      chunk_mask.unsqueeze(2).to_broadcast([P, CH_BLK, P]), ALU.mult).then_inc(S("v_blocks"), 1)
                    dve.wait_ge(S("att_mm"), m + 1)
                    dve.wait_ge(S("att_zeroed"), 2)
                    dve.copy_predicated(att[m % 2][:], intra, bank[2 + m % 2][:, 0:P]).then_inc(S("att_masked"), 1)

                masked(0)
                for m in range(BH * BLOCKS):
                    h, b = divmod(m, BLOCKS)
                    dve.wait_ge(S("state_mm"), m + 1)
                    for c in range(CH_BLK):
                        e = CH_BLK * m + c
                        kv = bank[4 + c // 4][:, (c % 4) * P:(c % 4 + 1) * P]
                        to = s_ring[:, (e + 1) % (2 * CH_BLK), :]
                        if c == CH_BLK - 1 and m:
                            dve.wait_ge(S("o_mm"), m)
                        if b == 0 and c == 0:
                            dve.tensor_copy(to, kv).then_inc(S("state_step"), 1)
                        else:
                            dve.wait_ge(S("state_step"), e)
                            dve.scalar_tensor_tensor(to, s_ring[:, e % (2 * CH_BLK), :], decay[:, h, CH_BLK * b + c:CH_BLK * b + c + 1],
                                                     kv, op0=ALU.mult, op1=ALU.add).then_inc(S("state_step"), 1)
                    if b == BLOCKS - 1:
                        dve.wait_ge(S("state_step"), CH_BLK * (m + 1))
                        dve.tensor_copy(s_fin[:, h, :], s_ring[:, (CH_BLK * (m + 1)) % (2 * CH_BLK), :]).then_inc(S("final_kept"), 1)
                    if m == 0:
                        dve.wait_ge(S("factor"), factors_before(1) + 6)
                        for c in range(CC):
                            dve.scalar_tensor_tensor(ckv[:, c, :], z[:, Z_CKV + c, :], gain[:, G_KV + c:G_KV + c + 1], t3[:],
                                                     op0=ALU.mult, op1=ALU.mult).then_inc(S("ckv_ready"), 1)
                        dve.tensor_tensor(rope_r[NOPE:P, :], cst[NOPE:P, C_ROPE:C_ROPE + NT], r[NOPE:P, :], ALU.mult) \
                            .then_inc(S("rope_ready"), 1)
                    if m == 1:
                        dve.wait_ge(S("ckv_hi_done"), 1)
                        dve.wait_ge(S("ckv_ready"), CC)
                        dve.tensor_tensor(ckv_lo[:], ckv[:], ckv_hi[:], ALU.subtract).then_inc(S("ckv_lo_done"), 1)
                    if m + 1 < BH * BLOCKS:
                        masked(m + 1)
                v_s = z[:, Z_I:Z_I + BH, SEQ:NT]
                for b in range(BATCH_D):
                    if b == 0:
                        dve.wait_ge(S("cq_summed"), 4)
                    else:
                        dve.wait_ge(S("v_spread"), b)
                    dve.tensor_tensor(v_diag[:], ident.unsqueeze(1).to_broadcast([P, BH, P]),
                                      v_s[:, :, b:b + 1].to_broadcast([P, BH, P]), ALU.mult).then_inc(S("v_diag_ready"), 1)
                    dve.wait_ge(S(f"st_loaded{b % 2}"), 16 * (b // 2 + 1))
                    dve.tensor_tensor(st[b % 2][:], st[b % 2][:], z[:, Z_F:Z_F + BH, SEQ + b:SEQ + b + 1].to_broadcast([P, BH, P]),
                                      ALU.mult).then_inc(S("s_decayed"), 1)
                    dve.wait_ge(S("v_spread"), b + 1)
                    if b:
                        dve.wait_ge(S("s_new"), b)
                    dve.tensor_tensor(s_tmp[:], bank[4 + b % 2][:].rearrange("p (h d) -> p h d", h=BH),
                                      k_all[:, :, SEQ + b:SEQ + b + 1].to_broadcast([P, BH, P]), ALU.mult).then_inc(S("kv_made"), 1)
                    dve.wait_ge(S("kv_made"), b + 1)
                    dve.tensor_tensor(st[b % 2][:], st[b % 2][:], s_tmp[:], ALU.add).then_inc(S("s_new"), 1)
                dve.wait_ge(S("os_mm"), BATCH_D)
                dve.tensor_copy(z[:, Z_Q:Z_Q + BH, SEQ:NT], bank[6][:, 0:BH * BATCH_D].rearrange("p (h b) -> p h b", h=BH)) \
                    .then_inc(S("os_kept"), 1)
                o_all = z[:, Z_Q:Z_Q + BH, :]
                dve.wait_ge(S("o_factor"), 1)
                dve.scalar_tensor_tensor(o_all, o_all, gain[:, G_OUT:G_OUT + 1], o_fac[:], op0=ALU.mult, op1=ALU.mult).then_inc(S("o_step"), 1)
                dve.wait_ge(S("o_step"), 1)
                dve.tensor_tensor(o_all, o_all, z[:, Z_G:Z_G + BH, :], ALU.mult).then_inc(S("o_step"), 1)
                dve.wait_ge(S("mix_hi_done"), 1)
                dve.wait_ge(S("o_step"), 2)
                dve.tensor_tensor(m_lo[:, BH:, :], o_all, m_hi[:, BH:, :], ALU.subtract).then_inc(S("mix_lo_done"), 1)

            def qkv():
                n0, g0 = U0["uq"], G0["uq"]
                pe_rows, sw_rows = slice(NOPE, NOPE + ROPE), slice(NOPE + ROPE, P)
                dve.wait_ge(S("mix_lo_done"), 1)
                dve.wait_ge(S("s_fin_stored"), 16)
                dve.wait_ge(S("rope_ready"), 1)
                for h in range(HEADS):
                    for hf in range(2):
                        ps = pair(g0 + h, hf)
                        if h < HEADS - 1:
                            dve.wait_ge(S("q_mm"), 2 * h + hf + 1)
                        else:
                            dve.wait_ge(S("half_done"), 2 * (n0 + 2) + hf + 1)
                        if 2 * h + hf >= 2:
                            dve.wait_ge(S("q_ready"), 2 * h + hf - 1)
                        dve.tensor_tensor(q_t[0:NOPE, h, half[hf]], ps[0:NOPE, :], r[0:NOPE, half[hf]], ALU.mult).then_inc(S("q_part"), 1)
                        dve.tensor_tensor(t1[pe_rows, half[hf]], ps[pe_rows, :], rope_r[pe_rows, half[hf]], ALU.mult).then_inc(S("q_part"), 1)
                        dve.tensor_tensor(t2[pe_rows, half[hf]], ps[sw_rows, :], rope_r[sw_rows, half[hf]], ALU.mult).then_inc(S("drained"), 1)
                        dve.wait_ge(S("drained"), 2 * (g0 + h) + hf + 1)
                        dve.tensor_tensor(q_t[pe_rows, h, half[hf]], t1[pe_rows, half[hf]], t2[pe_rows, half[hf]], ALU.add) \
                            .then_inc(S("q_ready"), 1)
                    if h in (2, 5, 7):
                        prefetch(n0 + (2, 5, 7).index(h))
                for t in range(BLOCKS):
                    if t < BLOCKS - 1:
                        dve.wait_ge(S("v_mm"), t + 1)
                    else:
                        dve.wait_ge(S("half_done"), 2 * (U0["ukv"] + UKV_UNITS))
                    dve.tensor_copy(v_t[:, t, :], bank[4 + t][:]).then_inc(S("v_kept"), 1)
                for u in range(UKV_UNITS):
                    prefetch(U0["ukv"] + u)

            def attention():
                dve.wait_ge(S("q_s_cleared"), 1)
                dve.wait_ge(S("q_lat_mm"), 1)
                dve.tensor_copy(q_s[:, :, 0:CC, :].rearrange("p b c h -> p c h b"),
                                bank[1][:, 0:CC * HEADS * BATCH_D].rearrange("p (c h b) -> p c h b", c=CC, h=HEADS)) \
                    .then_inc(S("q_s_ready"), 1)
                for j in range(GRP):
                    dve.tensor_copy(q_s[ROPE * j:ROPE * (j + 1), :, CC + j, :].rearrange("p b h -> p h b"),
                                    q_t[NOPE:NOPE + ROPE, :, SEQ:NT]).then_inc(S("q_s_ready"), 1)
                dve.memset(s_all[0:G_ROWS, GRP * P:GRP * P + 1], NEG).then_inc(S("s_cleared"), 1)
                dve.wait_ge(S("own_mm"), 1)
                dve.tensor_copy(own[0:HEADS, :], bank[3][0:HEADS, 0:BATCH_D]).then_inc(S("own_kept"), 1)
                causal = cst[:, C_CAUSAL:C_CAUSAL + P]

                def split(slots, width, k, n):
                    dve.wait_ge(S("c_hi_done"), n + 1)
                    dve.tensor_tensor(c_lo[n % SPLITS][:, :, 0:width], slots[k % RING][:], c_hi[n % SPLITS][:, :, 0:width], ALU.subtract) \
                        .then_inc(S("c_lo_done"), 1)

                def queries(i):
                    dve.wait_ge(S("q_win_hi"), i + 1)
                    dve.tensor_tensor(q_win[:, :, 2 * G_ROWS - HEADS:2 * G_ROWS], q_s[:, i],
                                      q_win[:, :, G_ROWS - HEADS:G_ROWS], ALU.subtract).then_inc(S("q_win_ready"), 1)

                def prompt(i, t):
                    if 1 <= t < 5:
                        b = t - 1
                        dve.wait_ge(S("s_mm"), i + 1)
                        s = score_at[b]
                        dve.tensor_tensor(s[:, b * P:(b + 1) * P], s[:, b * P:(b + 1) * P], causal, ALU.add).then_inc(S("s_masked"), 1)
                        dve.wait_ge(S("s_masked"), BLOCKS * i + b + 1)
                        dve.reduce_max(mx_p[:, 0, b:b + 1], s, AX.X).then_inc(S("max_taken"), 1)
                    if t == 4:
                        dve.wait_ge(S("max_taken"), BLOCKS * (i + 1))
                        if i:
                            dve.wait_ge(S("p_exp"), BLOCKS * i)
                        dve.tensor_scalar(mx_p[:, 1, :], mx_p[:, 0, :], -SM_SCALE, None, ALU.mult).then_inc(S("max_scaled"), 1)
                    if t == 9:
                        dve.wait_ge(S("p_exp"), BLOCKS * (i + 1))
                        dve.reciprocal(sum_p[:, 1, :], sum_p[:, 0, :]).then_inc(S("sum_inverse"), 1)
                        dve.wait_ge(S("sum_inverse"), i + 1)
                        for b in range(BLOCKS):
                            p = prob[:, tri(b):tri(b + 1), :]
                            dve.tensor_scalar(p, p, sum_p[:, 1, b:b + 1], None, ALU.mult).then_inc(S("p_ready"), 1)
                    if t == 15:
                        rows = slice(i % 2 * VDIM, (i % 2 + 1) * VDIM)
                        dve.wait_ge(S("oa_hi_done"), i + 1)
                        dve.tensor_tensor(m_lo[rows, i // 2, 0:SEQ], bank[4][rows, :], m_hi[rows, i // 2, 0:SEQ], ALU.subtract) \
                            .then_inc(S("oa_lo_done"), 1)

                def softmax(i, d):
                    if d == 1:
                        dve.wait_ge(S("s_lo_kept"), i + 1)
                        if i:
                            dve.wait_ge(S("s_exp"), i)
                        else:
                            dve.wait_ge(S("s_cleared"), 1)
                            dve.wait_ge(S("own_kept"), 1)
                        dve.tensor_tensor(s_all[0:G_ROWS, 0:GRP * P], bank[i % 2][0:G_ROWS, :], s_lo[0:G_ROWS, :], ALU.add).then_inc(S("s_added"), 1)
                        dve.tensor_copy(s_all[0:HEADS, GRP * P:GRP * P + 1], own[0:HEADS, i:i + 1]).then_inc(S("s_own"), 1)
                        dve.wait_ge(S("s_added"), i + 1)
                        dve.wait_ge(S("s_own"), i + 1)
                        dve.reduce_max(mx[0:G_ROWS, :], s_all[0:G_ROWS, :], AX.X).then_inc(S("mx_taken"), 1)
                    if d == 3:
                        dve.wait_ge(S("mx_turned"), i + 1)
                        dve.reduce_max(mx_row[0:1, :], bank[3][0:1, 0:G_ROWS].rearrange("p (g h) -> p h g", h=HEADS), AX.X).then_inc(S("mx_reduced"), 1)
                        dve.wait_ge(S("mx_reduced"), i + 1)
                        dve.tensor_copy(mx_rep[0:1, :].rearrange("p (g h) -> p g h", h=HEADS),
                                        mx_row[0:1, :].unsqueeze(1).to_broadcast([1, N_GRP, HEADS])).then_inc(S("mx_copied"), 1)
                    if d == 4:
                        dve.wait_ge(S("mx_spread"), i + 1)
                        dve.tensor_scalar(shift[0:G_ROWS, :], bank[3][0:G_ROWS, 64:65], -SM_SCALE, None, ALU.mult).then_inc(S("shift_ready"), 1)
                    if d == 7:
                        dve.wait_ge(S("p_hi_kept"), 2 * i + 2)
                        dve.tensor_tensor(p_t[i % 2][:, :, :, HEADS:2 * HEADS], p_turned, p_t[i % 2][:, :, :, 0:HEADS], ALU.subtract) \
                            .then_inc(S("p_t_ready"), 1)
                        dve.reciprocal(inv[i % 2][0:2 * HEADS, :], bank[3][0:2 * HEADS, 320:321]).then_inc(S("p_t_ready"), 1)

                def result(i, e):
                    if e == JOBS_SEQ:
                        dve.wait_ge(S("pv_done"), i + 1)
                        dve.wait_ge(S("p_t_ready"), 2 * i + 2)
                        if i:
                            dve.wait_ge(S("o_turned"), i)
                        dve.tensor_scalar(o_sb[0:2 * HEADS, :], bank[2][0:2 * HEADS, 0:CC * P], inv[i % 2][0:2 * HEADS, :], None, ALU.mult) \
                            .then_inc(S("o_sb_kept"), 1)
                    if e == JOBS_SEQ + 5:
                        dve.wait_ge(S("o_turned"), i + 1)
                        dve.tensor_copy(o_lat[:, :, :, i], bank[3][:, 0:CC * HEADS].rearrange("p (c h) -> p c h", c=CC)).then_inc(S("o_lat_ready"), 1)

                queries(0)
                for k in range(S_JOBS + LAG):
                    if k < S_JOBS:
                        split(s_raw, S_W, k, s_job(k))
                        prompt(*divmod(k, JOBS_SEQ))
                    if k >= LAG:
                        split(v_raw, KV_LORA, k - LAG, v_job(k - LAG))
                    if JOBS_SEQ <= k < S_JOBS + JOBS_SEQ:
                        softmax(k // JOBS_SEQ - 1, k % JOBS_SEQ + 1)
                    if k >= LAG + JOBS_SEQ:
                        result((k - LAG) // JOBS_SEQ - 1, (k - LAG) % JOBS_SEQ + JOBS_SEQ)
                    if k % JOBS_SEQ == 0 and 0 < k < S_JOBS:
                        queries(k // JOBS_SEQ)
                for e in range(JOBS_SEQ, JOBS_SEQ + 6):
                    result(BATCH_D - 1, e)
                for i in range(HEADS):
                    rows = slice(i % 2 * VDIM, (i % 2 + 1) * VDIM)
                    dve.wait_ge(S("oa_hi_done"), 2 * HEADS)
                    dve.tensor_tensor(m_lo[rows, i // 2, SEQ:NT], bank[0][rows, i * BATCH_D:(i + 1) * BATCH_D],
                                      m_hi[rows, i // 2, SEQ:NT], ALU.subtract).then_inc(S("oa_lo_done"), 1)

            def conv():
                n0, g0 = U0["c"], G0["c"]
                dve.wait_ge(S("drained"), 2 * g0)
                dve.memset(v_ext[:, 0:2], 0.0).then_inc(S("v_padded"), 1)

                def chunk(j0, count, i):
                    st = None if isinstance(i, int) else Step(i, 3)
                    j = j0
                    jj = j if st is None else j + i
                    n, g = n0 + 3 * j, g0 + 3 * j
                    nn, gg = n0 + 3 * jj, g0 + 3 * jj
                    tap = [gain[:, bass.ds(G_CONV + KC * k + jj, 1)] for k in range(3)]
                    if st is None:
                        factor_ready(READS["c"])
                        dve.wait_ge(S("v_padded"), 1)

                    def drain(u, to):
                        for hf in range(2):
                            dve.wait_ge(S("half_done"), 2 * (nn + u) + hf + 1)
                            dve.tensor_tensor(to[:, half[hf]], pair(g + u, hf), r[:, half[hf]], ALU.mult).then_inc(S("drained"), 1)

                    if st is not None:
                        dve.wait_ge(S("mix_lo_done"), jj + 1)
                    drain(0, t1)
                    prefetch(n, st)
                    drain(1, t3)
                    dve.wait_ge(S("drained"), 2 * (gg + 2))
                    if st is not None:
                        dve.wait_ge(S("conv_kept"), 2 * jj)
                    for hf in range(2):
                        dve.tensor_tensor(v_ext[:, 2 + hf * HALF:2 + (hf + 1) * HALF], t1[:, half[hf]], t3[:, half[hf]], ALU.mult) \
                            .then_inc(S("v_ready"), 1)
                    prefetch(n + 1, st)
                    dve.wait_ge(S("v_ready"), 2 * jj + 2)
                    if st is None:
                        dve.wait_ge(S("conv_st_loaded"), 16)
                    y, y_s = t2[:, 0:SEQ], t2[:, SEQ:NT]
                    dve.tensor_scalar(y, v_ext[:, 0:SEQ], tap[0], None, ALU.mult).then_inc(S("tap_done"), 1)
                    dve.tensor_scalar(y_s, conv_st[:, jj, 0, :], tap[0], None, ALU.mult).then_inc(S("tap_done"), 1)
                    dve.wait_ge(S("tap_done"), 6 * jj + 2)
                    dve.scalar_tensor_tensor(y, v_ext[:, 1:1 + SEQ], tap[1], y, op0=ALU.mult, op1=ALU.add).then_inc(S("tap_done"), 1)
                    dve.scalar_tensor_tensor(y_s, conv_st[:, jj, 1, :], tap[1], y_s, op0=ALU.mult, op1=ALU.add).then_inc(S("tap_done"), 1)
                    dve.wait_ge(S("tap_done"), 6 * jj + 4)
                    dve.scalar_tensor_tensor(y, v_ext[:, 2:2 + SEQ], tap[2], y, op0=ALU.mult, op1=ALU.add).then_inc(S("tap_done"), 1)
                    dve.scalar_tensor_tensor(y_s, v_ext[:, 2 + SEQ:2 + NT], tap[2], y_s, op0=ALU.mult, op1=ALU.add).then_inc(S("tap_done"), 1)
                    dve.wait_ge(S("tap_done"), 6 * jj + 6)
                    drain(2, t3)
                    dve.wait_ge(S("drained"), 2 * (gg + 3))
                    dve.tensor_tensor(t1[:], t3[:], t2[:], ALU.mult).then_inc(S("c_gated"), 1)
                    prefetch(n + 2, st)
                    dve.wait_ge(S("mix_hi_done"), jj + 2)
                    dve.tensor_tensor(m_lo[:, jj, :], t1[:], m_hi[:, jj, :], ALU.subtract).then_inc(S("mix_lo_done"), 1)

                over(dve, C_PEEL, KC, 1, chunk)

            dve.wait_ge(S("x_loaded"), 16)
            dve.wait_ge(S("gain_loaded"), 16)
            logit = [gain[:, G_LB + BH * k:G_LB + BH * (k + 1)] for k in range(3)]
            dve.tensor_tensor(lb[:, 3, :], logit[0], logit[1], ALU.max).then_inc(S("lb_max"), 1)
            dve.wait_ge(S("lb_max"), 1)
            dve.tensor_tensor(lb[:, 3, :], lb[:, 3, :], logit[2], ALU.max).then_inc(S("lb_max"), 1)
            dve.wait_ge(S("lb_max"), 2)
            for k in range(3):
                dve.tensor_tensor(lb[:, k, :], logit[k], lb[:, 3, :], ALU.subtract).then_inc(S("lb_step"), 1)
            for d in range(KC):
                chunk_dve(0, d, d)
            for n in range(3):
                split_lo(n)
            dve.wait_ge(S("lb_exp"), 1)
            dve.tensor_tensor(lb[:, 3, :], lb[:, 0, :], lb[:, 1, :], ALU.add).then_inc(S("lb_step"), 1)
            dve.wait_ge(S("lb_step"), 4)
            dve.tensor_tensor(lb[:, 3, :], lb[:, 3, :], lb[:, 2, :], ALU.add).then_inc(S("lb_step"), 1)
            dve.wait_ge(S("lb_step"), 5)
            dve.reciprocal(lb[:, 3, :], lb[:, 3, :]).then_inc(S("lb_step"), 1)
            dve.wait_ge(S("lb_step"), 6)
            dve.tensor_tensor(lb[:, 2, :], lb[:, 0, :], lb[:, 3, :], ALU.mult).then_inc(S("lb_step"), 1)
            dve.wait_ge(S("lb_step"), 7)
            dve.tensor_scalar(lb[:, 3, :], lb[:, 2, :], -1.0, 1.0, ALU.mult, ALU.add).then_inc(S("lb_step"), 1)
            dve.wait_ge(S("lb_step"), 8)
            ffn("ffn0")
            ab_in()
            hgrn()
            qkv()
            attention()
            out_projection("ab_out", 2)
            ffn("ffn1")
            ffn("ffn2")
            conv()
            out_projection("c_out", 5)
            ffn("ffn3")
            factor_ready(6)
            dve.wait_ge(S("x_added"), 2 * 6 * KC)
            for d in range(KC):
                dve.scalar_tensor_tensor(x[:, d, :], x[:, d, :], gain[:, G_FINAL + d:G_FINAL + d + 1], r[:], op0=ALU.mult, op1=ALU.mult) \
                    .then_inc(S("y_ready"), 1)

        @block.tensor
        def _(pe):
            mm = nc.tensor.matmul

            def stream_ready(res):
                def wait_chunk(c, hf):
                    pe.wait_ge(S("h_lo_done"), 16 * res + 2 * c + hf + 1)
                return wait_chunk

            def ffn(name):
                n0, g0, res, no = U0[name], G0[name], READS[name], FFN_NO[name]

                def gate_up(f0, count, i):
                    st = None if isinstance(i, int) else Step(i, 2 * count)
                    for f in range(f0, f0 + count):
                        ff = f if st is None else f + i * count
                        for u in range(2):
                            first = st is None and f == 0 and u == 0
                            if g0 + 2 * f + u >= 3:
                                group_free(g0 + 2 * ff + u)
                            unit_ready(n0 + 2 * ff + u)
                            multiply((n0 + 2 * f + u) % 3, g0 + 2 * f + u, h_hi, h_lo, 0, KC, True, True,
                                     stream_ready(res) if first else None)
                            if first:
                                norm_sum(res)

                over(pe, GATE_PEEL, FC, 3, gate_up)
                n0 += GATE_UNITS
                g0 += GATE_UNITS

                def down(d0, count, i):
                    st = None if isinstance(i, int) else Step(i, 3 * count)
                    for d in range(d0, d0 + count):
                        dd = d if st is None else d + i * count
                        group_free(g0 + dd)
                        for u in range(DOWN_U):
                            unit_ready(n0 + 3 * dd + u)
                            if st is None and d == 0 and u == 0:
                                pe.wait_ge(S("a_lo_done"), (no + 1) * 2 * FC - 2)
                            if st is None and d == 0 and u == 2:
                                pe.wait_ge(S("a_lo_done"), (no + 1) * 2 * FC)
                            multiply((n0 + 3 * d + u) % 3, g0 + d, a_hi, a_lo, 8 * u, min(8, FC - 8 * u), u == 0, u == 2)

                over(pe, OUT_PEEL, KC, 3, down, tail(name))

            def in_columns(name, count_units, peel, per):
                n0, g0, res = U0[name], G0[name], READS[name]

                def column(u0, count, i):
                    st = None if isinstance(i, int) else Step(i, count)
                    for u in range(u0, u0 + count):
                        uu = u if st is None else u + i * count
                        group_free(g0 + uu)
                        unit_ready(n0 + uu)
                        first = st is None and u == 0
                        multiply((n0 + u) % 3, g0 + u, h_hi, h_lo, 0, KC, True, True, stream_ready(res) if first else None)
                        if first:
                            norm_sum(res)

                over(pe, peel, count_units, per, column)

            def out_projection(name, mixed):
                n0, g0 = U0[name], G0[name]

                def column(d0, count, i):
                    st = None if isinstance(i, int) else Step(i, count)
                    for d in range(d0, d0 + count):
                        dd = d if st is None else d + i * count
                        group_free(g0 + dd)
                        unit_ready(n0 + dd)
                        multiply((n0 + d) % 3, g0 + d, m_hi, m_lo, 0, KC, True, True,
                                 mixed if st is None and d == 0 else None)

                over(pe, OUT_PEEL, KC, 3, column)

            def ab_in():
                in_columns("ab", AB_UNITS, Z_PEEL, 3)
                g0 = G0["ab"]
                for k, chunks in enumerate((range(QC), range(QC, QC + CC))):
                    pe.wait_ge(S("c_squared"), chunks[-1] + 1)
                    if k == 1:
                        pe.wait_ge(S("log_taken"), factors_before(1) + 4)
                    for hf in range(2):
                        for c in chunks:
                            sq = squares[:, c, half[hf]] if c < 4 else acc[:, half[hf]]
                            last = mm(bank[6 + hf][:, 0:HALF], ones, sq, start=c == chunks[0], stop=c == chunks[-1])
                        last.then_inc(S("cq_summed"), 1)

            def hgrn():
                g0 = G0["ab"]

                def scores(m):
                    h, b = divmod(m, BLOCKS)
                    if m >= 2:
                        pe.wait_ge(S("kv_kept"), m - 1)
                        pe.wait_ge(S("att_masked"), m - 1)
                    nc.tensor.transpose(bank[m % 2][:, 0:P], kd[:, h, o_block(h, b)], ident)
                    nc.tensor.transpose(bank[m % 2][:, P:2 * P], z[:, Z_I + h, o_block(h, b)], ident).then_inc(S("kv_transposed"), 1)
                    mm(bank[2 + m % 2][:, 0:P], ke[:, h, o_block(h, b)], qe[:, h, o_block(h, b)], start=True, stop=True) \
                        .then_inc(S("att_mm"), 1)

                pe.wait_ge(S("drained"), 2 * (g0 + AB_UNITS))
                pe.wait_ge(S("gates_ready"), 5)
                scores(0)
                for m in range(BH * BLOCKS):
                    h, b = divmod(m, BLOCKS)
                    pe.wait_ge(S("v_blocks"), m + 1)
                    if m:
                        pe.wait_ge(S("state_step"), CH_BLK * m)
                    for k in range(2):
                        last = mm(bank[4 + k][:], kdv[m % 2][:, 0, :], v_blk[m % 2][:, 4 * k:4 * k + 4, :], start=True, stop=True)
                    last.then_inc(S("state_mm"), 1)
                    if m + 1 < BH * BLOCKS:
                        scores(m + 1)
                    pe.wait_ge(S("att_masked"), m + 1)
                    if m == 0:
                        pe.wait_ge(S("factor"), factors_before(1) + 6)
                    if m >= 2:
                        pe.wait_ge(S("o_kept"), m - 1)
                    out = bank[6 + m % 2][:, 0:P]
                    mm(out, kdv[m % 2][:, 1, :], att[m % 2][:], start=True, stop=False)
                    for c in range(1 if b == 0 else 0, CH_BLK):
                        e = CH_BLK * m + c
                        if e:
                            pe.wait_ge(S("state_step"), e)
                        cols = slice(b * P + c * CHUNK, b * P + (c + 1) * CHUNK)
                        last = mm(out[:, c * CHUNK:(c + 1) * CHUNK], s_ring[:, e % (2 * CH_BLK), :], qe[:, h, cols],
                                  start=False, stop=c == CH_BLK - 1)
                    last.then_inc(S("o_mm"), 1)
                pe.wait_ge(S("state_step"), CH_BLK * BH * BLOCKS)
                pe.wait_ge(S("o_kept"), BH * BLOCKS)
                for b in range(BATCH_D):
                    pe.wait_ge(S("v_diag_ready"), b + 1)
                    if b >= 2:
                        pe.wait_ge(S("kv_made"), b - 1)
                    mm(bank[4 + b % 2][:], ones, v_diag[:], start=True, stop=True).then_inc(S("v_spread"), 1)
                    pe.wait_ge(S("s_new"), b + 1)
                    for h in range(BH):
                        at_o = h * BATCH_D + b
                        last = mm(bank[6][:, at_o:at_o + 1], st[b % 2][:, h, :], z[:, Z_Q + h, SEQ + b:SEQ + b + 1], start=True, stop=True)
                    last.then_inc(S("os_mm"), 1)
                pe.wait_ge(S("o_squared"), 1)
                for h in range(BH):
                    for hf in range(2):
                        mm(bank[2 * h + hf][:, 0:HALF], ones, k_all[:, h, half[hf]], start=True, stop=True).then_inc(S("o_summed"), 1)

            def qkv():
                n0, g0 = U0["uq"], G0["uq"]
                pe.wait_ge(S("cq_lo_done"), QC)
                pe.wait_ge(S("o_log"), 2 * BH)
                for h in range(HEADS):
                    if h >= 3:
                        group_free(g0 + h)
                    unit_ready(n0 + (QC * h + QC - 1) // 8)
                    for hf in range(2):
                        out = pair(g0 + h, hf)
                        for c in range(QC):
                            u, t = divmod(QC * h + c, 8)
                            wh, wl = w_hi[(n0 + u) % 3][:, t, :], w_lo[(n0 + u) % 3][:, t, :]
                            xh, xl = cq_hi[:, c, half[hf]], cq_lo[:, c, half[hf]]
                            mm(out, wh, xh, start=c == 0, stop=False)
                            mm(out, wh, xl, start=False, stop=False)
                            last = mm(out, wl, xh, start=False, stop=c == QC - 1)
                            if t == 7:
                                last.then_inc(S("half_done"), 1)
                        if h < HEADS - 1:
                            last.then_inc(S("q_mm"), 1)
                n0 = U0["ukv"]
                unit_ready(n0 + UKV_UNITS - 1)
                pe.wait_ge(S("ckv_lo_done"), 1)
                w = [(w_hi[(n0 + c) % 3], w_lo[(n0 + c) % 3]) for c in range(CC)]
                pe.wait_ge(S("drained"), 2 * (g0 + HEADS))
                for h in range(HEADS):
                    if h >= 4:
                        pe.wait_ge(S("k_kept"), HEADS + h - 3)
                    for c in range(CC):
                        out, xh, xl = bank[h % 4][:], ckv_hi[:, c, 0:SEQ], ckv_lo[:, c, 0:SEQ]
                        mm(out, w[c][0][:, h, :], xh, start=c == 0, stop=False)
                        mm(out, w[c][0][:, h, :], xl, start=False, stop=False)
                        last = mm(out, w[c][1][:, h, :], xh, start=False, stop=c == CC - 1)
                    last.then_inc(S("k_done"), 1)
                for t in range(BLOCKS):
                    tok = slice(t * P, (t + 1) * P)
                    for c in range(CC):
                        out, xh, xl = bank[4 + t][:], ckv_hi[:, c, tok], ckv_lo[:, c, tok]
                        wh, wl = (w[c][k][:, :, NOPE:NOPE + VDIM] for k in range(2))
                        mm(out, xh, wh, start=c == 0, stop=False)
                        one = mm(out, xl, wh, start=False, stop=False)
                        last = mm(out, xh, wl, start=False, stop=c == CC - 1)
                        if t == BLOCKS - 1:
                            one.then_inc(S("half_done"), 1)
                            last.then_inc(S("half_done"), 1)
                    if t < BLOCKS - 1:
                        last.then_inc(S("v_mm"), 1)

            def attention():
                pe.wait_ge(S("w_uk_loaded"), 16)
                pe.wait_ge(S("k_kept"), 2 * HEADS)
                pe.wait_ge(S("q_ready"), 2 * HEADS)
                for c in range(CC):
                    for h in range(HEADS):
                        at_q = (c * HEADS + h) * BATCH_D
                        last = mm(bank[1][:, at_q:at_q + BATCH_D], w_uk[:, h, c * P:(c + 1) * P], q_t[0:NOPE, h, SEQ:NT],
                                  start=True, stop=True)
                last.then_inc(S("q_lat_mm"), 1)
                pe.wait_ge(S("q_s_ready"), 1 + GRP)
                for b in range(BATCH_D):
                    out = bank[3][0:HEADS, b:b + 1]
                    for c in range(CC):
                        mm(out, q_s[:, b, c, :], ckv[:, c, SEQ + b:SEQ + b + 1], start=c == 0, stop=False)
                    last = mm(out, q_s[NOPE:NOPE + ROPE, b, CC + 2, :], k_pe[NOPE:NOPE + ROPE, SEQ + b:SEQ + b + 1], start=False, stop=True)
                last.then_inc(S("own_mm"), 1)
                pe.wait_ge(S("v_kept"), BLOCKS)

                def scores(k):
                    i, e = divmod(k, JOBS_SEQ)
                    n = s_job(k)
                    g, at_c = e // 2, e % 2 * JOB * P
                    hi, lo = c_hi[n % SPLITS], c_lo[n % SPLITS]
                    if e == 0:
                        pe.wait_ge(S("q_win_ready"), i + 1)
                        if i == 1:
                            pe.wait_ge(S("q_s_ready"), 1 + GRP)
                        if i >= 2:
                            pe.wait_ge(S("s_added"), i - 1)
                    pe.wait_ge(S("c_lo_done"), n + 1)
                    win = slice((G_ROWS - HEADS) - HEADS * g, (G_ROWS - HEADS) - HEADS * g + P)
                    out = bank[i % 2][:, at_c:at_c + JOB * P].rearrange("p (j t) -> p j t", j=JOB)
                    for c in range(CC):
                        for x_part, moving in enumerate((hi, lo)):
                            mm(out, q_win[:, c, win], moving[:, :, c * P:(c + 1) * P], start=e == 0 and c == 0 and x_part == 0, stop=False)
                    for q in range(GRP):
                        rows = slice(ROPE * q, ROPE * (q + 1))
                        for moving in (hi, lo):
                            last = mm(out[:, :, rows], q_win[:, CC + q, win], moving[:, :, CC * P:S_W], start=False,
                                      stop=e == JOBS_SEQ - 1 and q == GRP - 1 and moving is lo)
                    last.then_inc(S("job_done"), 1)

                def values(k):
                    i, e = divmod(k, JOBS_SEQ)
                    n = v_job(k)
                    hi, lo = c_hi[n % SPLITS], c_lo[n % SPLITS]
                    out = bank[2][0:2 * HEADS, 0:KV_LORA]
                    if e == 0:
                        pe.wait_ge(S("p_t_ready"), 2 * i + 2)
                        if i:
                            pe.wait_ge(S("o_sb_kept"), i)
                    pe.wait_ge(S("c_lo_done"), n + 1)
                    for j in range(JOB):
                        g, page = divmod(JOB * e + j, GRP)
                        for moving in (hi, lo):
                            last = mm(out, p_t[i % 2][:, page, g, :], moving[:, j, 0:KV_LORA], start=e == 0 and j == 0 and moving is hi, stop=False)
                    last.then_inc(S("job_done"), 1)
                    if e == JOBS_SEQ - 1:
                        pe.wait_ge(S("self_kept"), i + 1)
                        mm(out, p_own[i % 2][0:1, :], self_row[0:1, :], start=False, stop=True).then_inc(S("pv_done"), 1)

                def prompt(i, t):
                    if t == 0:
                        if i:
                            pe.wait_ge(S("pt_kept"), 3 * i)
                        for b in range(BLOCKS):
                            last = mm(score_at[b], q_t[0:NOPE + ROPE, i, b * P:(b + 1) * P], k_t[0:NOPE + ROPE, i, 0:(b + 1) * P],
                                      start=True, stop=True)
                        last.then_inc(S("s_mm"), 1)
                    if t == 10:
                        pe.wait_ge(S("p_ready"), BLOCKS * (i + 1))
                        for e in range(10):
                            last = nc.tensor.transpose(bank[5 + e // 4][:, (e % 4) * P:(e % 4 + 1) * P], prob[:, e, :], ident)
                            if e in (3, 7, 9):
                                last.then_inc(S("p_transposed"), 1)
                    if t == 14:
                        pe.wait_ge(S("pt_kept"), 3 * (i + 1))
                        if i:
                            pe.wait_ge(S("oa_lo_done"), i)
                        vals = slice(i // 2 * P, (i // 2 + 1) * P)
                        for b in range(BLOCKS):
                            for k in range(b + 1):
                                last = mm(bank[4][:, b * P:(b + 1) * P], v_t[:, k, vals], prob_t[:, tri(b) + k, :], start=k == 0, stop=k == b)
                        last.then_inc(S("o_a_mm"), 1)

                def softmax(i, d):
                    if d == 2:
                        pe.wait_ge(S("mx_taken"), i + 1)
                        if i == 0:
                            pe.wait_ge(S("own_kept"), 1)
                        if i >= 2:
                            pe.wait_ge(S("o_lat_ready"), i - 1)
                        mm(bank[3][0:1, 0:G_ROWS], mx[0:G_ROWS, :], ident[0:G_ROWS, 0:G_ROWS], start=True, stop=True).then_inc(S("mx_turned"), 1)
                    if d == 3:
                        pe.wait_ge(S("mx_copied"), i + 1)
                        mm(bank[3][0:G_ROWS, 64:65], mx_rep[0:1, :], ones[0:1, 0:1], start=True, stop=True).then_inc(S("mx_spread"), 1)
                    if d == 5:
                        pe.wait_ge(S("s_exp"), i + 1)
                        for j in range(GRP):
                            nc.tensor.transpose(bank[3][:, j * G_ROWS:(j + 1) * G_ROWS], p_all[0:G_ROWS, j * P:(j + 1) * P], ident[0:G_ROWS, 0:G_ROWS])
                        nc.tensor.transpose(bank[3][0:1, 256:320], p_all[0:G_ROWS, GRP * P:GRP * P + 1], ident[0:G_ROWS, 0:G_ROWS])
                        mm(bank[3][0:2 * HEADS, 320:321], sel[0:G_ROWS, :], row_sum[0:G_ROWS, :], start=True, stop=True).then_inc(S("p_turned"), 1)
                    if d == 9:
                        pe.wait_ge(S("p_t_ready"), 2 * i + 2)
                        for c in range(CC):
                            last = nc.tensor.transpose(bank[3][0:1, c * P:(c + 1) * P], ckv[:, c, SEQ + i:SEQ + i + 1], ident)
                        last.then_inc(S("self_turned"), 1)

                def result(i, e):
                    if e == JOBS_SEQ + 4:
                        pe.wait_ge(S("o_sb_kept"), i + 1)
                        pe.wait_ge(S("self_kept"), min(i + 2, BATCH_D))
                        for c in range(CC):
                            last = mm(bank[3][:, c * HEADS:(c + 1) * HEADS], o_sb[0:2 * HEADS, c * P:(c + 1) * P], sel[0:2 * HEADS, 0:HEADS],
                                      start=True, stop=True)
                        last.then_inc(S("o_turned"), 1)

                for k in range(S_JOBS + LAG):
                    if k < S_JOBS:
                        scores(k)
                        prompt(*divmod(k, JOBS_SEQ))
                    if k >= LAG:
                        values(k - LAG)
                    if JOBS_SEQ <= k < S_JOBS + JOBS_SEQ:
                        softmax(k // JOBS_SEQ - 1, k % JOBS_SEQ + 1)
                    if k >= LAG + JOBS_SEQ:
                        result((k - LAG) // JOBS_SEQ - 1, (k - LAG) % JOBS_SEQ + JOBS_SEQ)
                result(BATCH_D - 1, JOBS_SEQ + 4)
                pe.wait_ge(S("w_uv_loaded"), 16)
                pe.wait_ge(S("o_lat_ready"), BATCH_D)
                for i in range(HEADS):
                    pr_heads = slice(i // 2 * 2, i // 2 * 2 + 2)
                    for c in range(CC):
                        last = mm(bank[0][:, i * BATCH_D:(i + 1) * BATCH_D], w_uv[:, c, pr_heads, :].rearrange("p h v -> p (h v)"),
                                  o_lat[:, c, i, :], start=c == 0, stop=c == CC - 1)
                last.then_inc(S("os_a_mm"), 1)


            def ab_mixed(c, hf):
                if c == 0 and hf == 0:
                    pe.wait_ge(S("mix_lo_done"), 1)
                    pe.wait_ge(S("oa_lo_done"), 2 * HEADS)

            def c_mixed(c, hf):
                pe.wait_ge(S("mix_lo_done"), c + 2)

            pe.wait_ge(S("cst_loaded"), 16)
            ffn("ffn0")
            ab_in()
            hgrn()
            qkv()
            attention()
            out_projection("ab_out", ab_mixed)
            ffn("ffn1")
            ffn("ffn2")
            in_columns("c", C_UNITS, 3, 3)
            out_projection("c_out", c_mixed)
            ffn("ffn3")
            norm_sum(6)


def units(w):
    k, m = w.shape
    n = -(-k // (8 * P))
    full = np.zeros((n * 8 * P, m), w.dtype)
    full[:k] = w
    return full.reshape(n, 8, P, m // P, P).transpose(3, 0, 2, 1, 4).reshape(-1, P, UNIT)


def by_chunk(v):
    v = np.asarray(v)
    return np.moveaxis(v.reshape(v.shape[:-1] + (-1, P)), -1, 0)


def ffn_units(i, l, s):
    gate, up = (units(i[n][l, s]) for n in ("w_ffn_gate", "w_ffn_up"))
    both = np.stack([gate, up], axis=1).reshape(-1, P, UNIT)
    return [both, units(i["w_ffn_down"][l, s])]


def rope_columns(w):
    out = np.zeros((w.shape[0], P), w.dtype)
    out[:, 64:96] = w
    out[:, 96:128] = np.roll(w, ROPE // 2, axis=1)
    return out


def lay_out(i):
    w_in = i["w_in_ab"][0]
    cuts = np.cumsum([Q_LORA, KV_LORA, ROPE, BH * DK, BH * DK, BH * DK])
    c_q, c_kv, k_pe, q_b, f_b, i_b, g_b = np.split(w_in, cuts, axis=1)
    uq = i["w_uq"][0].reshape(Q_LORA, HEADS, NOPE + ROPE)
    uq = np.concatenate([uq, np.roll(uq[:, :, NOPE:], ROPE // 2, axis=2)], axis=2)
    uq = uq.reshape(QC, P, HEADS, P).transpose(2, 0, 1, 3).reshape(UQ_UNITS, 8, P, P).transpose(0, 2, 1, 3).reshape(UQ_UNITS, P, UNIT)
    ukv = i["w_ukv"][0].reshape(CC, P, UNIT)
    c_in = i["w_in_c"][0].reshape(D_MODEL, 3, D_MODEL)
    bg, cg, u = (units(c_in[:, k]) for k in range(3))
    c_in = np.stack([cg, u, bg], axis=1).reshape(-1, P, UNIT)
    stream = (ffn_units(i, 0, 0) + [units(t) for t in (q_b, g_b, f_b, i_b, c_q, c_kv, rope_columns(k_pe))] + [uq, ukv]
              + [units(i["w_out_ab"][0])] + ffn_units(i, 0, 1) + ffn_units(i, 1, 0) + [c_in, units(i["w_out_c"][0])]
              + ffn_units(i, 1, 1))
    w = np.concatenate(stream)
    assert w.shape[0] == N_UNITS
    gain = np.zeros((P, G_W), np.float32)
    gain[:, G_NORM:G_NORM + 48] = by_chunk(i["norm_g"]).reshape(P, 48)
    gain[:, G_FINAL:G_FINAL + KC] = by_chunk(i["final_norm_g"])
    gain[:, G_Q:G_Q + QC] = by_chunk(i["g_q_lora"][0])
    gain[:, G_KV:G_KV + CC] = by_chunk(i["g_kv_lora"][0])
    gain[:, G_LB:G_LB + 3 * BH] = by_chunk(i["hgrn_lower_bound"]).reshape(P, 3 * BH)
    gain[:, G_OUT:G_OUT + 1] = by_chunk(i["g_hgrn_out"][0])
    gain[:, G_CONV:G_CONV + 3 * KC] = by_chunk(i["w_conv_c"][0]).reshape(P, 3 * KC)
    cst = np.zeros((P, C_W), np.float32)
    cst[:, C_IDENT:C_IDENT + P] = np.eye(P)
    cst[:, C_ONES:C_ONES + P] = 1
    pos = np.concatenate([np.arange(SEQ), np.full(BATCH_D, PAGE * PAGES)]).astype(np.float32)
    inv = np.power(np.float32(10000.0), -np.arange(0, ROPE, 2, dtype=np.float32) / np.float32(ROPE)).astype(np.float32)
    ang = (inv[:, None] * pos[None, :]).astype(np.float32)
    cos, sin = np.cos(ang), np.sin(ang)
    cst[64:96, C_ROPE:C_ROPE + NT] = np.concatenate([cos, cos])
    cst[96:128, C_ROPE:C_ROPE + NT] = np.concatenate([-sin, sin])
    t = np.arange(P)
    cst[:, C_CAUSAL:C_CAUSAL + P] = np.where(t[None, :] <= t[:, None], 0.0, NEG)
    cst[:, C_INTRA:C_INTRA + P] = (t[:, None] <= t[None, :]) & (t[:, None] // CHUNK == t[None, :] // CHUNK)
    cst[:, C_CHUNK:C_CHUNK + CH_BLK] = t[:, None] // CHUNK == np.arange(CH_BLK)[None, :]
    cst[:, C_EPS] = EPS
    cst[:, C_SEL:C_SEL + 2 * HEADS] = t[:, None] % HEADS == np.arange(2 * HEADS)[None, :] % HEADS
    scan = np.broadcast_to((np.arange(SEQ) % CHUNK != 0).astype(np.float32), (P, SEQ))
    x = np.concatenate([i["x_prompt"].reshape(SEQ, D_MODEL), i["x_sample"].reshape(BATCH_D, D_MODEL)])
    lat = i["cache_ckv"][0]
    lat_t = lat.reshape(POOL, PAGE, CC, P).transpose(0, 3, 2, 1).reshape(POOL, P, CC * PAGE)
    keys = i["cache_kpe"][0].reshape(POOL, GRP, ROPE, ROPE).transpose(0, 1, 3, 2).reshape(POOL, P, ROPE)
    cache = np.concatenate([lat_t, keys, lat], axis=2)
    w_ukv = i["w_ukv"][0].reshape(KV_LORA, HEADS, NOPE + VDIM)
    return {
        "x": by_chunk(x).transpose(0, 2, 1), "w": w, "gain": gain, "cst": cst, "scan": scan, "cache": cache,
        "pages": i["page_table"].reshape(1, -1).astype(np.int32),
        "state": i["state_hgrn"][0].transpose(0, 2, 1, 3),
        "conv_st": by_chunk(i["state_conv"][0]).transpose(0, 3, 2, 1),
        "w_uk": w_ukv[:, :, :NOPE].transpose(2, 1, 0), "w_uv": w_ukv[:, :, NOPE:].reshape(CC, P, HEADS, VDIM).transpose(1, 0, 2, 3),
    }


OUTS = {"y": (P, KC, NT), "ckv": (P, CC, NT), "k_pe": (ROPE, NT), "state_p": (P, BH, P), "state_s": (BATCH_D, P, BH, P),
        "conv_p": (P, KC, 2), "conv_s": (P, KC, 2, BATCH_D)}


def kernel(**inputs):
    import concourse.bacc as bacc
    from concourse.bass_utils import run_bass_kernel_spmd

    i = {k: np.asarray(v) for k, v in inputs.items()}
    arrays = {f"in_{k}": np.ascontiguousarray(v) for k, v in lay_out(i).items()}
    nc = bacc.Bacc("TRN2", target_bir_lowering=False, num_devices=1)
    dram = {k[3:]: nc.dram_tensor(k, a.shape, mybir.dt.from_np(a.dtype), kind="ExternalInput").ap() for k, a in arrays.items()}
    for k, shape in OUTS.items():
        dram[k] = nc.dram_tensor(f"out_{k}", shape, F32, kind="ExternalOutput").ap()
    build(nc, dram)
    got = run_bass_kernel_spmd(nc, [arrays], core_ids=[0]).results[0]
    y, ckv, k_pe, state_p, state_s, conv_p, conv_s = (got[f"out_{k}"] for k in OUTS)
    y = y.transpose(2, 1, 0).reshape(NT, D_MODEL)
    ckv = ckv.transpose(2, 1, 0).reshape(NT, KV_LORA)
    k_pe = k_pe.T
    return (y[None, :SEQ], y[SEQ:, None],
            ckv[None, None, :SEQ], k_pe[None, None, :SEQ], ckv[None, SEQ:, None], k_pe[None, SEQ:, None],
            state_p.transpose(1, 0, 2)[None, None], state_s.transpose(0, 2, 1, 3)[None],
            conv_p.transpose(2, 1, 0).reshape(1, 1, 2, D_MODEL),
            conv_s.transpose(3, 2, 1, 0).reshape(1, BATCH_D, 2, D_MODEL))
```
